# Optimizing a Trainium2 kernel written in Bass

```python
import jax, jax.numpy as jnp
from jax import lax
import numpy as np

D_MODEL = 1024
BATCH = 1
SEQ = 256
DEPTH = 2

HEAD_DIM = 64
N_HEADS_MOBA = 4
N_HEADS_FOX = 4
N_HEADS_MLA = 4
N_HEADS_DIL = 4
W_MOBA = N_HEADS_MOBA * HEAD_DIM
W_FOX = N_HEADS_FOX * HEAD_DIM
W_DIL = N_HEADS_DIL * HEAD_DIM

MOBA_BLOCK = 256
MOBA_TOPK = 3
MOBA_Q_CHUNK = 64
Q_BLOCK = 128

MLA_Q_RANK = 192
MLA_KV_RANK = 128
MLA_NOPE_DIM = 64
MLA_ROPE_DIM = 32
MLA_V_DIM = 64
MLA_Q_UP = N_HEADS_MLA * (MLA_NOPE_DIM + MLA_ROPE_DIM)
MLA_KV_UP = N_HEADS_MLA * (MLA_NOPE_DIM + MLA_V_DIM)
W_MLA = N_HEADS_MLA * MLA_V_DIM

DILATED_CONFIGS = ((128, 1), (512, 4), (2048, 16))
ROPE_THETA = 10000.0
RMS_EPS = 1e-6
D_FF = -(-8 * D_MODEL // (3 * 256)) * 256

IN_SIZES = (3 * W_MOBA, 3 * W_FOX, N_HEADS_FOX, MLA_Q_RANK, MLA_KV_RANK, MLA_ROPE_DIM, 3 * W_DIL)
D_IN = 3 * W_MOBA + 3 * W_FOX + N_HEADS_FOX + MLA_Q_RANK + MLA_KV_RANK + MLA_ROPE_DIM + 3 * W_DIL
SPLIT_POINTS = (
    3 * W_MOBA,
    3 * W_MOBA + 3 * W_FOX,
    3 * W_MOBA + 3 * W_FOX + N_HEADS_FOX,
    3 * W_MOBA + 3 * W_FOX + N_HEADS_FOX + MLA_Q_RANK,
    3 * W_MOBA + 3 * W_FOX + N_HEADS_FOX + MLA_Q_RANK + MLA_KV_RANK,
    3 * W_MOBA + 3 * W_FOX + N_HEADS_FOX + MLA_Q_RANK + MLA_KV_RANK + MLA_ROPE_DIM,
)
MIX_WIDTH = W_MOBA + W_FOX + W_MLA + W_DIL


def rmsnorm(x, g):
    xf = x.astype(jnp.float32)
    y = xf * lax.rsqrt(jnp.mean(xf * xf, axis=-1, keepdims=True) + RMS_EPS)
    return (y * g.astype(jnp.float32)).astype(x.dtype)

def rope_tables(positions, dim):
    inv_freq = ROPE_THETA ** (-jnp.arange(0, dim, 2, dtype=jnp.float32) / dim)
    ang = positions.astype(jnp.float32)[..., None] * inv_freq
    return jnp.cos(ang), jnp.sin(ang)

def apply_rope(x, cos, sin):
    x1, x2 = jnp.split(x.astype(jnp.float32), 2, axis=-1)
    c = cos[:, None]
    s = sin[:, None]
    return jnp.concatenate([x1 * c - x2 * s, x2 * c + x1 * s], axis=-1).astype(x.dtype)

def to_heads(t, n_heads):
    b, s, _ = t.shape
    return t.reshape(b, s, n_heads, -1).transpose(0, 2, 1, 3)

def from_heads(t):
    b, h, s, d = t.shape
    return t.transpose(0, 2, 1, 3).reshape(b, s, h * d)

def pad_seq(t, new_len):
    pad = new_len - t.shape[2]
    return jnp.pad(t, ((0, 0), (0, 0), (0, pad), (0, 0)))

def blocked_causal_attention(q, k, v, scale, cum=None):
    b, h, s, dq = q.shape
    nq = s // Q_BLOCK
    qb = jnp.moveaxis(q.reshape(b, h, nq, Q_BLOCK, dq), 2, 0)
    starts = jnp.arange(nq, dtype=jnp.int32) * Q_BLOCK
    key_pos = jnp.arange(s, dtype=jnp.int32)

    def body(xs):
        if cum is None:
            qi, start = xs
        else:
            qi, start, ci = xs
        sc = jnp.einsum('bhqd,bhkd->bhqk', qi, k, preferred_element_type=jnp.float32) * scale
        if cum is not None:
            sc = sc + (ci[..., None] - cum[:, :, None, :])
        q_pos = start + jnp.arange(Q_BLOCK, dtype=jnp.int32)
        sc = jnp.where(key_pos[None, :] <= q_pos[:, None], sc, -jnp.inf)
        p = jax.nn.softmax(sc, axis=-1)
        return jnp.einsum('bhqk,bhkd->bhqd', p.astype(v.dtype), v)

    if cum is None:
        xs = (qb, starts)
    else:
        xs = (qb, starts, jnp.moveaxis(cum.reshape(b, h, nq, Q_BLOCK), 2, 0))
    out = lax.map(body, xs)
    return jnp.moveaxis(out, 0, 2).reshape(b, h, s, v.shape[-1])

def moba_attention(q, k, v):
    b, h, s, d = q.shape
    sp = -(-s // MOBA_BLOCK) * MOBA_BLOCK
    q, k, v = pad_seq(q, sp), pad_seq(k, sp), pad_seq(v, sp)
    nb = sp // MOBA_BLOCK
    scale = d ** -0.5
    kb = k.reshape(b, h, nb, MOBA_BLOCK, d)
    vb = v.reshape(b, h, nb, MOBA_BLOCK, d)
    k_mean = jnp.mean(kb.astype(jnp.float32), axis=3)
    gate = jnp.einsum('bhsd,bhnd->bhsn', q.astype(jnp.float32), k_mean)
    q_blk = jnp.arange(sp, dtype=jnp.int32) // MOBA_BLOCK
    past = jnp.arange(nb, dtype=jnp.int32)[None, :] < q_blk[:, None]
    gate = jnp.where(past, gate, -jnp.inf)
    k_sel = min(MOBA_TOPK, nb)
    _, sel = lax.top_k(gate, k_sel)
    sel_valid = jnp.arange(k_sel, dtype=jnp.int32)[None, :] < q_blk[:, None]

    nc = sp // MOBA_Q_CHUNK
    qc = jnp.moveaxis(q.reshape(b, h, nc, MOBA_Q_CHUNK, d), 2, 0)
    selc = jnp.moveaxis(sel.reshape(b, h, nc, MOBA_Q_CHUNK, k_sel), 2, 0)
    validc = sel_valid.reshape(nc, MOBA_Q_CHUNK, k_sel)
    starts = jnp.arange(nc, dtype=jnp.int32) * MOBA_Q_CHUNK
    b_idx = jnp.arange(b)[:, None, None, None]
    h_idx = jnp.arange(h)[None, :, None, None]
    n_sel = k_sel * MOBA_BLOCK

    def body(xs):
        qi, si, vi, start = xs
        own = start // MOBA_BLOCK
        k_own = lax.dynamic_index_in_dim(kb, own, axis=2, keepdims=False)
        v_own = lax.dynamic_index_in_dim(vb, own, axis=2, keepdims=False)
        q_pos = start + jnp.arange(MOBA_Q_CHUNK, dtype=jnp.int32)
        k_pos = own * MOBA_BLOCK + jnp.arange(MOBA_BLOCK, dtype=jnp.int32)
        s_own = jnp.einsum('bhqd,bhkd->bhqk', qi, k_own, preferred_element_type=jnp.float32) * scale
        s_own = jnp.where(k_pos[None, :] <= q_pos[:, None], s_own, -jnp.inf)
        k_g = kb[b_idx, h_idx, si]
        v_g = vb[b_idx, h_idx, si]
        s_g = jnp.einsum('bhqd,bhqjkd->bhqjk', qi, k_g, preferred_element_type=jnp.float32) * scale
        s_g = jnp.where(vi[None, None, :, :, None], s_g, -jnp.inf)
        s_all = jnp.concatenate([s_g.reshape(b, h, MOBA_Q_CHUNK, n_sel), s_own], axis=-1)
        p = jax.nn.softmax(s_all, axis=-1).astype(v.dtype)
        p_g = p[..., :n_sel].reshape(b, h, MOBA_Q_CHUNK, k_sel, MOBA_BLOCK)
        p_own = p[..., n_sel:]
        return (jnp.einsum('bhqjk,bhqjkd->bhqd', p_g, v_g)
                + jnp.einsum('bhqk,bhkd->bhqd', p_own, v_own))

    out = lax.map(body, (qc, selc, validc, starts))
    return jnp.moveaxis(out, 0, 2).reshape(b, h, sp, d)[:, :, :s]

def dilated_branch(q, k, v, window, dilation):
    b, h, s, d = q.shape
    L = window // dilation
    seg = dilation * L
    sp = -(-s // seg) * seg
    n = sp // dilation
    nb = n // L
    scale = d ** -0.5

    def to_sub(t):
        t = pad_seq(t, sp).reshape(b, h, n, dilation, d).transpose(0, 1, 3, 2, 4)
        return t.reshape(b, h, dilation, nb, L, d)

    def with_prev(t):
        prev = jnp.concatenate([jnp.zeros_like(t[:, :, :, :1]), t[:, :, :, :-1]], axis=3)
        return jnp.concatenate([prev, t], axis=4)

    qs = to_sub(q)
    k2 = with_prev(to_sub(k))
    v2 = with_prev(to_sub(v))
    sc = jnp.einsum('bhrnqd,bhrnkd->bhrnqk', qs, k2, preferred_element_type=jnp.float32) * scale
    i = jnp.arange(L)[:, None]
    m = jnp.arange(2 * L)[None, :]
    diff = L + i - m
    blk = jnp.arange(nb)[:, None, None]
    mask = (diff >= 0) & (diff <= L) & ((m >= L) | (blk > 0))
    sc = jnp.where(mask, sc, -jnp.inf)
    lse = jax.nn.logsumexp(sc, axis=-1)
    p = jnp.exp(sc - lse[..., None]).astype(v.dtype)
    o = jnp.einsum('bhrnqk,bhrnkd->bhrnqd', p, v2)
    o = o.reshape(b, h, dilation, n, d).transpose(0, 1, 3, 2, 4).reshape(b, h, sp, d)[:, :, :s]
    lse = lse.reshape(b, h, dilation, n).transpose(0, 1, 3, 2).reshape(b, h, sp)[:, :, :s]
    return o, lse

def dilated_mixture(q, k, v):
    outs, lses = [], []
    for window, dilation in DILATED_CONFIGS:
        o, l = dilated_branch(q, k, v, window, dilation)
        outs.append(o.astype(jnp.float32))
        lses.append(l)
    wts = jax.nn.softmax(jnp.stack(lses, axis=0), axis=0)
    out = jnp.sum(wts[..., None] * jnp.stack(outs, axis=0), axis=0)
    return out.astype(q.dtype)

def first_inputs(seed: int = 0) -> dict:
    key = jax.random.key(seed)
    ks = jax.random.split(key, 16)
    f32 = jnp.float32

    def nrm(k, shape, fan_in):
        return jax.random.normal(k, shape, f32) * (fan_in ** -0.5)

    def gain(k, dim):
        return 1.0 + 0.02 * jax.random.normal(k, (DEPTH, dim), f32)

    x = jax.random.normal(ks[0], (BATCH, SEQ, D_MODEL), f32)
    positions = jnp.broadcast_to(jnp.arange(SEQ, dtype=jnp.int32)[None, :], (BATCH, SEQ))
    return {
        "x": x,
        "positions": positions,
        "w_in": nrm(ks[1], (DEPTH, D_MODEL, D_IN), D_MODEL),
        "b_forget": 0.1 * jax.random.normal(ks[2], (DEPTH, N_HEADS_FOX), f32),
        "g_mla_q": gain(ks[3], MLA_Q_RANK),
        "w_mla_q_up": nrm(ks[4], (DEPTH, MLA_Q_RANK, MLA_Q_UP), MLA_Q_RANK),
        "g_mla_kv": gain(ks[5], MLA_KV_RANK),
        "w_mla_kv_up": nrm(ks[6], (DEPTH, MLA_KV_RANK, MLA_KV_UP), MLA_KV_RANK),
        "w_out": nrm(ks[7], (DEPTH, MIX_WIDTH, D_MODEL), MIX_WIDTH),
        "g_pre_mix": gain(ks[8], D_MODEL),
        "g_post_mix": gain(ks[9], D_MODEL),
        "w_gate": nrm(ks[10], (DEPTH, D_MODEL, D_FF), D_MODEL),
        "w_up": nrm(ks[11], (DEPTH, D_MODEL, D_FF), D_MODEL),
        "w_down": nrm(ks[12], (DEPTH, D_FF, D_MODEL), D_FF),
        "g_pre_ffn": gain(ks[13], D_MODEL),
        "g_post_ffn": gain(ks[14], D_MODEL),
    }

def first_block(x, positions, w_in, b_forget, g_mla_q, w_mla_q_up, g_mla_kv, w_mla_kv_up, w_out,
              g_pre_mix, g_post_mix, w_gate, w_up, w_down, g_pre_ffn, g_post_ffn):
    cos_h, sin_h = rope_tables(positions, HEAD_DIM)
    cos_r, sin_r = rope_tables(positions, MLA_ROPE_DIM)
    b, s, _ = x.shape
    for l in range(DEPTH):
        h = rmsnorm(x, g_pre_mix[l])
        z = jnp.einsum('bsd,de->bse', h, w_in[l])
        z_moba, z_fox, z_fg, z_cq, z_ckv, z_kr, z_dil = jnp.split(z, SPLIT_POINTS, axis=-1)

        qa, ka, va = [to_heads(t, N_HEADS_MOBA) for t in jnp.split(z_moba, 3, axis=-1)]
        qa, ka = apply_rope(qa, cos_h, sin_h), apply_rope(ka, cos_h, sin_h)
        o_moba = moba_attention(qa, ka, va)

        qb, kb, vb = [to_heads(t, N_HEADS_FOX) for t in jnp.split(z_fox, 3, axis=-1)]
        log_f = jax.nn.log_sigmoid(z_fg.astype(jnp.float32) + b_forget[l].astype(jnp.float32))
        cum = jnp.cumsum(log_f, axis=1).transpose(0, 2, 1)
        o_fox = blocked_causal_attention(qb, kb, vb, HEAD_DIM ** -0.5, cum)

        c_q = rmsnorm(z_cq, g_mla_q[l])
        q_c = to_heads(jnp.einsum('bsr,re->bse', c_q, w_mla_q_up[l]), N_HEADS_MLA)
        q_nope, q_rope = q_c[..., :MLA_NOPE_DIM], q_c[..., MLA_NOPE_DIM:]
        c_kv = rmsnorm(z_ckv, g_mla_kv[l])
        kv = to_heads(jnp.einsum('bsr,re->bse', c_kv, w_mla_kv_up[l]), N_HEADS_MLA)
        k_nope, v_c = kv[..., :MLA_NOPE_DIM], kv[..., MLA_NOPE_DIM:]
        k_rope = apply_rope(z_kr[:, None], cos_r, sin_r)
        q_full = jnp.concatenate([q_nope, apply_rope(q_rope, cos_r, sin_r)], axis=-1)
        k_full = jnp.concatenate(
            [k_nope, jnp.broadcast_to(k_rope, (b, N_HEADS_MLA, s, MLA_ROPE_DIM))], axis=-1)
        o_mla = blocked_causal_attention(q_full, k_full, v_c, (MLA_NOPE_DIM + MLA_ROPE_DIM) ** -0.5)

        qd, kd, vd = [to_heads(t, N_HEADS_DIL) for t in jnp.split(z_dil, 3, axis=-1)]
        qd, kd = apply_rope(qd, cos_h, sin_h), apply_rope(kd, cos_h, sin_h)
        o_dil = dilated_mixture(qd, kd, vd)

        mix = jnp.concatenate([from_heads(o_moba), from_heads(o_fox), from_heads(o_mla),
                               from_heads(o_dil)], axis=-1)
        y = jnp.einsum('bse,ed->bsd', mix, w_out[l])
        x = x + rmsnorm(y, g_post_mix[l])

        h = rmsnorm(x, g_pre_ffn[l])
        f = jax.nn.silu(jnp.einsum('bsd,df->bsf', h, w_gate[l])) * jnp.einsum('bsd,df->bsf', h, w_up[l])
        f = jnp.einsum('bsf,fd->bsd', f, w_down[l])
        x = x + rmsnorm(f, g_post_ffn[l])
    return x


CHUNK = 64
D_FF_2 = 2816
CONV_W = D_MODEL
CONV_K = 3
CONV_GROUPS = 16
POOL_W = D_MODEL
POOL_WINDOWS = (2, 4, 8, 16)
POOL_GROUPS = len(POOL_WINDOWS)
POOL_GC = POOL_W // POOL_GROUPS
N_BRANCH = 2
IN_COLS = 3 * CONV_W + POOL_W + N_BRANCH * D_MODEL
EPS = 1e-6


def rms_norm(x, g):
    xf = x.astype(jnp.float32)
    y = xf * lax.rsqrt(jnp.mean(xf * xf, axis=-1, keepdims=True) + EPS)
    return (y * g.astype(jnp.float32)).astype(x.dtype)

def swiglu(h, w_gate_up, w_down):
    gu = h @ w_gate_up
    g, u = jnp.split(gu, 2, axis=-1)
    return (jax.nn.silu(g) * u) @ w_down

def causal_depthwise_conv(u, w):
    s = u.shape[1]
    u_pad = jnp.pad(u, ((0, 0), (CONV_K - 1, 0), (0, 0)))
    y = w[0] * u_pad[:, 0:s]
    for k in range(1, CONV_K):
        y = y + w[k] * u_pad[:, k:k + s]
    return y

def trailing_mean(u, win):
    s = u.shape[1]
    cs = jnp.cumsum(u, axis=1)
    cs_shift = jnp.pad(cs, ((0, 0), (win, 0), (0, 0)))[:, :s]
    count = jnp.minimum(jnp.arange(1, s + 1), win).astype(jnp.float32)
    return (cs - cs_shift) / count[None, :, None]

def pool_mixer(p, w_pg, b_pg, scale):
    b, s, _ = p.shape
    pf = p.astype(jnp.float32).reshape(b, s, POOL_GROUPS, POOL_GC)
    pooled = jnp.stack([trailing_mean(pf[:, :, gi], win) for gi, win in enumerate(POOL_WINDOWS)], axis=2)
    d = (pooled - pf).astype(p.dtype)
    y = jnp.einsum('bsgc,gcd->bsgd', d, w_pg) + b_pg
    return y.reshape(b, s, POOL_W) * scale

def hybrid_mixer(h, w_in, b_gate, conv_w, w_conv_out, w_pg, b_pg, pool_scale, w_pool_out, w_o):
    z = h @ w_in
    b_g, c_g, v, p, gates = jnp.split(
        z, [CONV_W, 2 * CONV_W, 3 * CONV_W, 3 * CONV_W + POOL_W], axis=-1)
    y_a = (b_g * causal_depthwise_conv(c_g * v, conv_w)) @ w_conv_out
    y_p = pool_mixer(p, w_pg, b_pg, pool_scale) @ w_pool_out
    g = jax.nn.sigmoid((gates + b_gate).astype(jnp.float32)).astype(h.dtype)
    g_a, g_p = jnp.split(g, N_BRANCH, axis=-1)
    return (g_a * y_a + g_p * y_p) @ w_o

def second_inputs(seed: int = 0) -> dict:
    key = jax.random.key(seed)
    ks = jax.random.split(key, 24)
    f32 = jnp.float32

    def nrm(k, shape, fan_in):
        return jax.random.normal(k, shape, f32) * (fan_in ** -0.5)

    def gain(k, shape):
        return 1.0 + 0.05 * jax.random.normal(k, shape, f32)

    L = DEPTH
    return {
        "x": jax.random.normal(ks[0], (BATCH, SEQ, D_MODEL), f32),
        "ffn1_pre": gain(ks[1], (L, D_MODEL)),
        "ffn1_post": gain(ks[2], (L, D_MODEL)),
        "ffn1_w_gate_up": nrm(ks[3], (L, D_MODEL, 2 * D_FF_2), D_MODEL),
        "ffn1_w_down": nrm(ks[4], (L, D_FF_2, D_MODEL), D_FF_2),
        "mix_pre": gain(ks[5], (L, D_MODEL)),
        "mix_post": gain(ks[6], (L, D_MODEL)),
        "w_in": nrm(ks[7], (L, D_MODEL, IN_COLS), D_MODEL),
        "b_gate": 0.01 * jax.random.normal(ks[8], (L, N_BRANCH * D_MODEL), f32),
        "conv_w": nrm(ks[9], (L, CONV_K, CONV_W), CONV_K),
        "w_conv_out": nrm(ks[10], (L, CONV_W, D_MODEL), CONV_W),
        "w_pool_group": nrm(ks[11], (L, POOL_GROUPS, POOL_GC, POOL_GC), POOL_GC),
        "b_pool_group": 0.01 * jax.random.normal(ks[12], (L, POOL_GROUPS, POOL_GC), f32),
        "pool_scale": gain(ks[13], (L, POOL_W)),
        "w_pool_out": nrm(ks[14], (L, POOL_W, D_MODEL), POOL_W),
        "w_o": nrm(ks[15], (L, D_MODEL, D_MODEL), D_MODEL),
        "ffn2_pre": gain(ks[16], (L, D_MODEL)),
        "ffn2_post": gain(ks[17], (L, D_MODEL)),
        "ffn2_w_gate_up": nrm(ks[18], (L, D_MODEL, 2 * D_FF_2), D_MODEL),
        "ffn2_w_down": nrm(ks[19], (L, D_FF_2, D_MODEL), D_FF_2),
    }

def second_block(x, ffn1_pre, ffn1_post, ffn1_w_gate_up, ffn1_w_down,
              mix_pre, mix_post, w_in, b_gate, conv_w, w_conv_out,
              w_pool_group, b_pool_group, pool_scale, w_pool_out, w_o,
              ffn2_pre, ffn2_post, ffn2_w_gate_up, ffn2_w_down):
    for l in range(DEPTH):
        h = swiglu(rms_norm(x, ffn1_pre[l]), ffn1_w_gate_up[l], ffn1_w_down[l])
        x = x + 0.5 * rms_norm(h, ffn1_post[l])
        h = hybrid_mixer(rms_norm(x, mix_pre[l]), w_in[l], b_gate[l], conv_w[l],
                         w_conv_out[l], w_pool_group[l], b_pool_group[l],
                         pool_scale[l], w_pool_out[l], w_o[l])
        x = x + rms_norm(h, mix_post[l])
        h = swiglu(rms_norm(x, ffn2_pre[l]), ffn2_w_gate_up[l], ffn2_w_down[l])
        x = x + 0.5 * rms_norm(h, ffn2_post[l])
    return x


def setup_inputs(seed=0):
    out = dict(first_inputs(seed))
    for name, value in second_inputs(seed + 1).items():
        if name != "x":
            out[name + "_2"] = value
    return out


def reference(
    x, positions, w_in, b_forget, g_mla_q, w_mla_q_up, g_mla_kv, w_mla_kv_up, w_out, g_pre_mix,
    g_post_mix, w_gate, w_up, w_down, g_pre_ffn, g_post_ffn, ffn1_pre_2, ffn1_post_2,
    ffn1_w_gate_up_2, ffn1_w_down_2, mix_pre_2, mix_post_2, w_in_2, b_gate_2, conv_w_2,
    w_conv_out_2, w_pool_group_2, b_pool_group_2, pool_scale_2, w_pool_out_2, w_o_2, ffn2_pre_2,
    ffn2_post_2, ffn2_w_gate_up_2, ffn2_w_down_2,
):
    x = first_block(
        x, positions, w_in, b_forget, g_mla_q, w_mla_q_up, g_mla_kv, w_mla_kv_up, w_out,
        g_pre_mix, g_post_mix, w_gate, w_up, w_down, g_pre_ffn, g_post_ffn,
    )
    return second_block(
        x, ffn1_pre_2, ffn1_post_2, ffn1_w_gate_up_2, ffn1_w_down_2, mix_pre_2, mix_post_2,
        w_in_2, b_gate_2, conv_w_2, w_conv_out_2, w_pool_group_2, b_pool_group_2, pool_scale_2,
        w_pool_out_2, w_o_2, ffn2_pre_2, ffn2_post_2, ffn2_w_gate_up_2, ffn2_w_down_2,
    )


_drawn_inputs = setup_inputs


def setup_inputs(seed=0):
    import zlib

    import numpy as np

    out = dict(_drawn_inputs(seed))
    spreads = {}
    factors = {'g_mla_q': 8.0,
     'g_mla_kv': 5.022,
     'ffn1_post_2': 3.288,
     'b_gate_2': 26.604,
     'b_pool_group_2': 8.0,
     'pool_scale_2': 2.949,
     'ffn2_pre_2': 2.682,
     'ffn2_post_2': 3.986}
    for name, (base, spread) in spreads.items():
        noise = np.random.default_rng([zlib.crc32(name.encode()), seed]).standard_normal(out[name].shape)
        drawn = base * np.exp(spread * noise) if base else spread * noise
        out[name] = __import__('jax').numpy.asarray(drawn.astype(out[name].dtype))
    for name, factor in factors.items():
        out[name] = (out[name] * factor).astype(out[name].dtype)
    return out
```

```python
from contextlib import ExitStack

import numpy as np

import concourse.bass as bass
from concourse import mybir

F32 = mybir.dt.float32
F32R = mybir.dt.float32r
BF16 = mybir.dt.bfloat16
I32 = mybir.dt.int32
ALU = mybir.AluOpType
ACT = mybir.ActivationFunctionType
AX_X = mybir.AxisListType.X

P = 128
S = 256
DM = 1024
NK = DM // P
DFF = 2816
FC = 256
NJ = DFF // FC
LAYERS = 2
H = 4
HD = 64
ROPE_D = 32
QR, KVR = 192, 128
QRH = QR // 2
EPS = 1e-6
NEG = 1.0e30
ROPE_THETA = 10000.0
WINDOWS = (2, 4, 8, 16)

C_MOBA, C_FOX = 0, 3 * H * HD
C_FG = 2 * 3 * H * HD
C_CQ = C_FG + H
C_CKV = C_CQ + QR
C_KR = C_CKV + KVR
C_DIL = C_KR + ROPE_D
D_IN = C_DIL + 3 * H * HD
NC1 = D_IN // 512
REM = D_IN - 512 * NC1
IN2 = 6 * DM
NC2 = IN2 // 512

SLOTS = 3
UNIT = 2048
SM_KV, SM_Q = NK * REM, NK * REM + 512
SLOTW = SM_Q + 2 * 384
U_IN, U_SMALL, U_OUT, U_FFN, U1 = 0, 10, 11, 15, 48
V_FFN1, V_IN, V_PG, V_PO, V_CO, V_WO, V_FFN2, U2 = 0, 33, 57, 60, 64, 68, 72, 105
BASE2 = LAYERS * U1
assert U1 % SLOTS == 0 and U2 % SLOTS == 0

PIECES = [(0, 0), (0, 1), (1, 0), (1, 1)]


def at(l, n, k):
    return l * n + k


class Unit:

    def __init__(self, base, per, l, k, i=0, step=0):
        self.slot = (base + k) % SLOTS
        self.done = l * per + i * step + (base + k + 1)
        self.turns = l * (per // SLOTS) + i * (step // SLOTS) + ((base + k) // SLOTS + 1)


def first_units(l):
    return lambda k, i=0, step=0: Unit(0, U1, l, k, i, step)


def second_units(l):
    return lambda k, i=0, step=0: Unit(BASE2, U2, l, k, i, step)


def build(nc, A, out):
    with ExitStack() as ctx:
        def sb(name, shape, dt=F32):
            return ctx.enter_context(nc.sbuf_tensor(name, shape, dt))

        def sem(name):
            return ctx.enter_context(nc.semaphore(name))

        Dp = ctx.enter_context(nc.psum_tensor("Dp", [P, 2048], F32))
        Gp = ctx.enter_context(nc.psum_tensor("Gp", [P, 1024], F32))
        Tp = ctx.enter_context(nc.psum_tensor("Tp", [P, 1024], F32))

        def D(t, c, n=512):
            return Dp[:, (2 * t + c) * 512:(2 * t + c) * 512 + n]

        def G(t, n=512):
            return Gp[:, t * 512:t * 512 + n]

        def T(b, n=512, p=P):
            return Tp[0:p, b * 512:b * 512 + n]

        def chunk_bank(c, t, n=512):
            return G(t, n) if c % 3 == 2 else D(c % 3, t, n)

        x = sb("x", [P, 2, DM])
        raw = [sb(f"raw{i}", [P, SLOTW]) for i in range(SLOTS)]
        whi = [sb(f"whi{i}", [P, SLOTW], F32R) for i in range(SLOTS)]
        wlo = [sb(f"wlo{i}", [P, SLOTW], F32R) for i in range(SLOTS)]
        a_hi = sb("a_hi", [P, NK, S], F32R)
        a_lo = sb("a_lo", [P, NK, S], F32R)
        b_hi = sb("b_hi", [P, NK, S], F32R)
        b_lo = sb("b_lo", [P, NK, S], F32R)
        f_hi = sb("f_hi", [P, 2, S], F32R)
        f_lo = sb("f_lo", [P, 2, S], F32R)
        stage = sb("stage", [P, 2, 512])
        inner = sb("inner", [P, 4, FC])
        gate, ffn = inner[:, 0:2, :], inner[:, 2:4, :]
        junk = inner[:, :, :].rearrange("p a n -> p (a n)").bitcast(BF16).rearrange("p (a n) -> p a n", a=4)
        gp = [sb(f"gp{i}", [P, DM]) for i in range(3)]
        gmla = gp[2][:, 0:QR + KVR]
        bfor = sb("bfor", [P, H])
        ident = sb("ident", [P, P])
        prm = sb("prm", [P, 160])
        cur = sb("cur", [P, 64])
        st = sb("st", [P, 96])
        causal = sb("causal", [P, S])
        dilm = sb("dilm", [P, S])
        dilc = sb("dilc", [P, S])
        upper = sb("upper", [P, 2, P])
        band = sb("band", [P, 4, 384])
        posi = sb("posi", [P, 2], I32)
        cosh = sb("cosh", [P, 2, 32])
        sinh = sb("sinh", [P, 2, 32])
        cosr = sb("cosr", [P, 2, 16])
        sinr = sb("sinr", [P, 2, 16])
        Z = sb("Z", [P, 14592])

        rows_a, rows_b = Z[:, 4096:4096 + P], Z[0:32, 4352:4352 + P]
        half = st[:, 0:2]
        ssx, rsx = st[:, 2:4], st[:, 4:6]
        ssy, sy, rsy = st[:, 8:12], st[:, 12:14], st[:, 14:16]
        ssm, rsm = st[:, 16:20], st[:, 20:24]
        fg = [st[:, 24 + 8 * i:32 + 8 * i].rearrange("p (t h) -> p t h", t=2) for i in range(5)]
        mx, nm, sums = st[:, 64:72], st[:, 72:80], st[:, 80:88]
        rec = st[:, 88:96]

        z = Z[:, 0:2 * D_IN].rearrange("p (t n) -> p t n", t=2)
        o0 = 2 * D_IN
        zq = Z[:, o0:o0 + 768].rearrange("p (t h d) -> p t h d", t=2, h=H)
        zk = Z[:, o0 + 768:o0 + 1536].rearrange("p (t h d) -> p t h d", t=2, h=H)
        vm = Z[:, o0 + 1536:o0 + 2048].rearrange("p (t h d) -> p t h d", t=2, h=H)
        o1 = o0 + 2048
        qT = Z[:, o1:o1 + 1024].rearrange("p (h s) -> p h s", h=H)
        kT = Z[:, o1 + 1024:o1 + 2048].rearrange("p (h s) -> p h s", h=H)
        o2 = o1 + 2048
        probs = [[Z[:, o2 + 1536 * i:o2 + 1536 * i + 512].rearrange("p (h s) -> p h s", h=H),
                  Z[:, o2 + 1536 * i + 512:o2 + 1536 * (i + 1)].rearrange("p (h s) -> p h s", h=H)]
                 for i in range(2)]
        o3 = o2 + 3072
        pT = [Z[:, o3 + 512 * i:o3 + 512 * (i + 1)].rearrange("p (h s) -> p h s", h=H) for i in range(3)]
        rt = [Z[:, o3 + 512 * i:o3 + 512 * (i + 1)] for i in range(2)]
        rt_dil = Z[:, o3 + 1536:o3 + 2048]
        rt_mla = Z[:, o3 + 1024:o3 + 1024 + 256]
        scratch = [Z[:, o2 + S * i:o2 + S * (i + 1)] for i in range(8)]
        dist, back, count = (scratch[i].bitcast(I32) for i in range(3))
        z2 = Z[:, 0:2 * IN2].rearrange("p (t n) -> p t n", t=2)
        bgate = Z[:, 2 * IN2:2 * IN2 + 2 * DM]

        def quarter(c, off):
            return z2[:, c, off:off + DM].rearrange("p (k s) -> p k s", k=4)

        loaded = [sem(f"loaded{i}") for i in range(SLOTS)]
        hi_done = sem("hi_done")
        split_done = sem("split_done")
        unit_used = sem("unit_used")
        x_loaded = sem("x_loaded")
        x_ready = sem("x_ready")
        par_loaded = sem("par_loaded")
        con = sem("con")
        tab = sem("tab")
        tab_act = sem("tab_act")
        iotas, mask_step, band_step = sem("iotas"), sem("mask_step"), sem("band_step")
        par_turned = sem("par_turned")
        par_ready = sem("par_ready")
        x_out = sem("x_out")
        short_loaded = sem("short_loaded")
        waited_pe, waited_pool = sem("waited_pe"), sem("waited_pool")

        class Use:

            def __init__(self, base, per, idx):
                self.base, self.per, self.idx = base, per, idx

            def round(self, l):
                return l * self.per + (self.base + self.idx)

        class Turn(Use):

            def __init__(self, sems, *use):
                Use.__init__(self, *use)
                self.turned, self.gained, self.hi, self.lo, self.squared, self.mean, self.rstd = sems

        class Ffn(Use):
            def __init__(self, sems, *use):
                Use.__init__(self, *use)
                self.gu, self.silu, self.f, self.turned, self.hi, self.lo, self.y = sems

        class Post(Use):

            def __init__(self, sems, *use):
                Use.__init__(self, *use)
                self.squared, self.sum, self.mean, self.rstd, self.scaled = sems

        gained_turn = [sem("in_" + n) for n in ("turned", "gained", "hi", "lo", "squared", "mean", "rstd")]
        plain_turn = [sem("out_turned"), None, sem("out_hi"), sem("out_lo"), None, None, None]
        ffn_sems = [sem("ffn_" + n) for n in ("gu", "silu", "f", "turned", "hi", "lo", "y")]
        post_sems = [sem("post_" + n) for n in ("squared", "sum", "mean", "rstd", "scaled")]

        class Proj:
            def __init__(self, n):
                self.t0, self.free0, self.free1 = sem(n + "_t0"), sem(n + "_free0"), sem(n + "_free1")

        p_in1, y_out1 = Proj("pin1"), sem("y_out1")
        p_in2 = Proj("pin2")
        t_mix1, t_ffn1 = (Turn(gained_turn, 0, 2, i) for i in range(2))
        t_f21, t_mix2, t_f22 = (Turn(gained_turn, 2 * LAYERS, 3, i) for i in range(3))
        t_att, t_gated = Turn(plain_turn, 0, 1, 0), Turn(plain_turn, LAYERS, 1, 0)
        f_1 = Ffn(ffn_sems, 0, 1, 0)
        f_21, f_22 = (Ffn(ffn_sems, LAYERS, 2, i) for i in range(2))
        n_mix1, n_ffn1 = (Post(post_sems, 0, 2, i) for i in range(2))
        n_f21, n_mix2, n_f22 = (Post(post_sems, 2 * LAYERS, 3, i) for i in range(3))

        gains_in = [sem("gains_in1"), sem("gains_in2")]
        cur_ready = [sem("cur_ready1"), sem("cur_ready2")]
        fox_staged = sem("fox_staged")
        fg_dve, fg_act, fg_sum, fg_put = sem("fg_dve"), sem("fg_act"), sem("fg_sum"), sem("fg_put")
        ml_sq, ml_pool, ml_norm = sem("ml_sq"), sem("ml_pool"), sem("ml_norm")
        ml_turned, ml_hi, ml_lo = sem("ml_turned"), sem("ml_hi"), sem("ml_lo")
        ml_q, ml_out0, ml_out1, ml_rope = sem("ml_q"), sem("ml_out0"), sem("ml_out1"), sem("ml_rope")
        moba_rope, dil_rope = sem("moba_rope"), sem("dil_rope")
        qk_turned, q_out, k_out = sem("qk_turned"), sem("q_out"), sem("k_out")
        s_done, masked, maxed, neg_max = sem("s_done"), sem("masked"), sem("maxed"), sem("neg_max")
        p_ready, dil_p, recd = sem("p_ready"), sem("dil_p"), sem("recd")
        p_turned, pT_act, pT_dve = sem("p_turned"), sem("pT_act"), sem("pT_dve")
        o_done, o_norm = sem("o_done"), sem("o_norm")
        u_done, biased, sig_done = sem("u_done"), sem("biased"), sem("sig_done")
        pooled, d_hi, d_lo = sem("pooled"), sem("d_hi"), sem("d_lo")
        pg_0, yp_f, yp_hi, yp_lo = sem("pg_0"), sem("yp_f"), sem("yp_hi"), sem("yp_lo")
        ub_turned, ub_out = sem("ub_turned"), sem("ub_out")
        conv, cv_hi, cv_lo = sem("conv"), sem("cv_hi"), sem("cv_lo")
        y_po, y_co, y_wo = sem("y_po"), sem("y_co"), sem("y_wo")
        po_gated, co_gated, mixed = sem("po_gated"), sem("co_gated"), sem("mixed")

        def x1(l, k):
            return l * 8 + 4 * (k + 1)

        def x2(l, k):
            return l * 12 + (LAYERS * 8 + 4 * (k + 1))

        def kinds():
            def heads(c0):
                return [lambda t, h, c=c0 + 256 * j: z[:, t, c + HD * h:c + HD * (h + 1)] for j in range(2)]

            def vals(c0):
                return lambda t, h: z[:, t, c0 + 512 + HD * h:c0 + 512 + HD * (h + 1)]

            mq, mk = heads(C_MOBA)
            dq, dk = heads(C_DIL)
            fd = HD + 2
            md = HD + ROPE_D
            return [
                ("fox", fd, HD ** -0.5, lambda t, h: zq[:, t, h, 0:fd], lambda t, h: zk[:, t, h, 0:fd],
                 vals(C_FOX), causal, C_FOX),
                ("moba", HD, HD ** -0.5, mq, mk, vals(C_MOBA), causal, C_MOBA),
                ("dil", HD, HD ** -0.5, dq, dk, vals(C_DIL), dilm, C_DIL),
                ("mla", md, md ** -0.5, lambda t, h: zq[:, t, h, :], lambda t, h: zk[:, t, h, :],
                 lambda t, h: vm[:, t, h, :], causal, C_FOX + 256),
            ]

        KINDS = kinds()
        MIX_COLS = [C_MOBA, C_MOBA + 128, C_FOX, C_FOX + 128, C_FOX + 256, C_FOX + 384, C_DIL, C_DIL + 128]

        def scores_bank(n, qt):
            if qt == 0:
                v = D(0, n % 2)
            else:
                v = Dp[:, 1024:2048] if n % 2 == 0 else Gp[:, :]
            return v

        def scores_view(n, qt):
            return scores_bank(n, qt).rearrange("p (h s) -> p h s", h=H)

        def heads_out(n, qt):
            return scores_bank(n, qt)[:, 0:H * HD].rearrange("p (h d) -> p h d", h=H)

        block = ctx.enter_context(nc.Block())

        @block.sync
        def _(sp):
            sp.dma_start(x[:, :, :], A["x"].rearrange("a (t p) d -> p (a t) d", p=P)).then_inc(x_loaded, 16)

            def put(unit, parts):
                sp.wait_ge(split_done, unit.done)
                for dst, src in parts:
                    sp.dma_start(dst, src).then_inc(loaded[unit.slot], 16)

            def rows(w):
                return w.rearrange("l (k p) n -> l p k n", p=P)

            def project(units, k, w, l, h, cols, i=0, step=0):
                u = units(k, i, step)
                r = raw[u.slot][:, 0:UNIT].rearrange("p (k n) -> p k n", k=4)
                put(u, [(r[:, 2 * e:2 * e + 2, :], w[l, :, 4 * h + 2 * e:4 * h + 2 * e + 2, cols])
                        for e in range(2)])

            def gate_up(units, k, wg, wu, l, h, gcols, ucols, i=0, step=0):
                u = units(k, i, step)
                r = raw[u.slot][:, 0:UNIT].rearrange("p (k g n) -> p k g n", k=4, g=2)
                put(u, [(r[:, :, 0, :], wg[l, :, 4 * h:4 * h + 4, gcols]),
                        (r[:, :, 1, :], wu[l, :, 4 * h:4 * h + 4, ucols])])

            def down(units, k, w, l, j, i=0, step=0):
                u = units(k, i, step)
                r = raw[u.slot][:, 0:UNIT].rearrange("p (k n) -> p k n", k=2)
                put(u, [(r[:, e:e + 1, :], w[l, :, j, e:e + 1, :]) for e in range(2)])

            def swiglu(units, k0, wg, wu, wd, l, off):
                wdr = wd.rearrange("l (j k p) n -> l p j k n", p=P, k=2)
                for j in range(2):
                    for h in range(2):
                        gate_up(units, k0 + 2 * j + h, wg, wu, l, h, slice(FC * j, FC * j + FC),
                                slice(off + FC * j, off + FC * j + FC))
                down(units, k0 + 4, wdr, l, 0)
                with sp.Fori(0, NJ - 2, 1) as i:
                    for h in range(2):
                        gate_up(units, k0 + 5 + h, wg, wu, l, h, bass.ds(i * FC + 2 * FC, FC),
                                bass.ds(i * FC + (off + 2 * FC), FC), i, 3)
                    down(units, k0 + 7, wdr, l, i + 1, i, 3)
                down(units, k0 + 3 * NJ - 1, wdr, l, NJ - 1)

            w_in, w_out = rows(A["w_in"]), rows(A["w_out"])
            w_g, w_u = rows(A["w_gate"]), rows(A["w_up"])
            with sp.Fori(0, LAYERS, 1) as l:
                units = first_units(l)
                for c in range(NC1):
                    for h in range(2):
                        project(units, U_IN + 2 * c + h, w_in, l, h, slice(512 * c, 512 * c + 512))
                u = units(U_SMALL)
                sp.wait_ge(split_done, u.done)
                sm = raw[u.slot]
                sp.dma_start(sm[:, 0:SM_KV].rearrange("p (k n) -> p k n", k=NK),
                             w_in[l, :, :, 512 * NC1:D_IN]).then_inc(short_loaded, 16)
                sp.dma_start(sm[:, SM_KV:SM_Q], A["w_mla_kv_up"][l]).then_inc(loaded[u.slot], 16)
                sp.dma_start(sm[0:QRH, SM_Q:SLOTW].rearrange("p (k n) -> p k n", k=2),
                             A["w_mla_q_up"].rearrange("l (k p) n -> l p k n", p=QRH)[l]
                             ).then_inc(loaded[u.slot], 16)
                for c in range(2):
                    for h in range(2):
                        project(units, U_OUT + 2 * c + h, w_out, l, h, slice(512 * c, 512 * c + 512))
                swiglu(units, U_FFN, w_g, w_u, A["w_down"], l, 0)

            w_in2, w_po, w_co, w_o = (rows(A[n]) for n in ("w_in_2", "w_pool_out_2", "w_conv_out_2", "w_o_2"))
            gu1, gu2 = rows(A["ffn1_w_gate_up_2"]), rows(A["ffn2_w_gate_up_2"])
            wpg = A["w_pool_group_2"].rearrange("l g (k p) n -> l p g k n", p=P)
            with sp.Fori(0, LAYERS, 1) as l:
                units = second_units(l)
                swiglu(units, V_FFN1, gu1, gu1, A["ffn1_w_down_2"], l, DFF)
                with sp.Fori(0, NC2 // 3, 1) as i:
                    for c in range(3):
                        for h in range(2):
                            project(units, V_IN + 2 * c + h, w_in2, l, h,
                                    bass.ds(i * 1536 + 512 * c, 512), i, 6)
                u = units(V_PG)
                r = raw[u.slot][:, 0:1024].rearrange("p (g k n) -> p g k n", g=2, k=2)
                put(u, [(r[:, g, :, :], wpg[l, :, g, :, :]) for g in range(2)])
                for g in range(2, 4):
                    u = units(V_PG + g - 1)
                    r = raw[u.slot][:, 0:512].rearrange("p (k n) -> p k n", k=2)
                    put(u, [(r[:, e:e + 1, :], wpg[l, :, g, e:e + 1, :]) for e in range(2)])
                for k0, w in ((V_PO, w_po), (V_CO, w_co), (V_WO, w_o)):
                    for c in range(2):
                        for h in range(2):
                            project(units, k0 + 2 * c + h, w, l, h, slice(512 * c, 512 * c + 512))
                swiglu(units, V_FFN2, gu2, gu2, A["ffn2_w_down_2"], l, DFF)

            for k in range(2):
                u = second_units(LAYERS - 1)(U2 + k)
                sp.wait_ge(split_done, u.done)
                sp.sem_inc(loaded[u.slot], 32)

            sp.wait_ge(x_ready, x2(LAYERS - 1, 3))
            sp.dma_start(out.rearrange("a (t p) d -> p (a t) d", p=P), x[:, :, :]).then_inc(x_out, 16)
            sp.wait_ge(x_out, 16)

        @block.gpsimd
        def _(pool):
            for j, n in enumerate(("g_pre_mix", "ffn1_pre_2", "g_pre_ffn", "mix_pre_2", "ffn2_pre_2")):
                pool.dma_start(rows_a[16 * j:16 * j + 16, :],
                               A[n].rearrange("l (k p) -> (l k) p", p=P)).then_inc(par_loaded, 16)
            pool.dma_start(rows_a[80:128, :], A["conv_w_2"].rearrange("l c (k p) -> (l c k) p", p=P)
                           ).then_inc(par_loaded, 16)
            pool.dma_start(rows_b[0:16, :], A["b_pool_group_2"].rearrange("l g (k p) -> (l g k) p", p=P)
                           ).then_inc(par_loaded, 16)
            pool.dma_start(rows_b[16:32, :], A["pool_scale_2"].rearrange("l (k p) -> (l k) p", p=P)
                           ).then_inc(par_loaded, 16)
            pool.dma_start(posi[:, :], A["positions"].rearrange("a (t p) -> p (a t)", p=P),
                           allow_slow_non_contiguous=True
                           ).then_inc(par_loaded, 16)
            pool.memset(ident[:, :], 0.0).then_inc(con, 1)
            pool.wait_ge(con, 1)
            pool.affine_select(out=ident[:, :], in_=ident[:, :], compare_op=ALU.not_equal, fill=1.0,
                               base=0, pattern=[[-1, P]], channel_multiplier=1).then_inc(con, 1)
            pool.memset(half[:, 0:1], -0.5).then_inc(con, 1)
            pool.memset(half[:, 1:2], -0.5).then_inc(con, 1)
            freq = (np.float32(ROPE_THETA) ** (-np.arange(0, HD, 2, dtype=np.float32) / np.float32(HD)))
            for j in range(32):
                pool.memset(Z[:, j:j + 1], float(freq[j])).then_inc(con, 1)
            def pow_half(dst, src, n, ready, value, done):
                pool.wait_ge(ready, value)
                pool.tensor_tensor(dst, src, half[:, 0:n], ALU.pow).then_inc(done, 1)

            def input_rstd(l, tn):
                pool.wait_ge(tn.squared, at(tn.round(l), 2, 2))
                pool.sem_inc(waited_pool, 1)
                pool.tensor_scalar(ssx, ssx, 1.0 / DM, EPS, ALU.mult, ALU.add).then_inc(tn.mean, 1)
                pow_half(rsx, ssx, 2, tn.mean, at(tn.round(l), 1, 1), tn.rstd)

            def output_rstd(l, pn, weight):
                pool.wait_ge(pn.squared, at(pn.round(l), 4, 4))
                s4 = ssy.rearrange("p (t c) -> p t c", c=2)
                pool.tensor_tensor(sy, s4[:, :, 0], s4[:, :, 1], ALU.add).then_inc(pn.sum, 1)
                pool.wait_ge(pn.sum, at(pn.round(l), 1, 1))
                pool.sem_inc(waited_pool, 1)
                w = weight ** -2
                pool.tensor_scalar(sy, sy, w / DM, w * EPS, ALU.mult, ALU.add).then_inc(pn.mean, 1)
                pow_half(rsy, sy, 2, pn.mean, at(pn.round(l), 1, 1), pn.rstd)

            with pool.Fori(0, LAYERS, 1) as l:
                input_rstd(l, t_mix1)
                pool.dma_start(gp[0][:, :], A["g_post_mix"][l].partition_broadcast(P)).then_inc(gains_in[0], 16)
                pool.dma_start(gp[1][:, :], A["g_post_ffn"][l].partition_broadcast(P)).then_inc(gains_in[0], 16)
                pool.dma_start(gmla[:, 0:QR], A["g_mla_q"][l].partition_broadcast(P)).then_inc(gains_in[0], 16)
                pool.dma_start(gmla[:, QR:QR + KVR], A["g_mla_kv"][l].partition_broadcast(P)
                               ).then_inc(gains_in[0], 16)
                pool.dma_start(bfor[:, :], A["b_forget"][l].partition_broadcast(P)).then_inc(gains_in[0], 16)
                pool.iota(dist, pattern=[[-1, S]], base=P, channel_multiplier=1).then_inc(iotas, 1)
                pool.iota(back, pattern=[[1, S]], base=0, channel_multiplier=-1).then_inc(iotas, 1)
                pool.iota(count, pattern=[[1, S]], base=1, channel_multiplier=0).then_inc(iotas, 1)
                pool.wait_ge(p_in1.free0, at(l, 6, 3 + 3))
                pool.wait_ge(p_in1.free1, at(l, 6, 3 + 3))
                pool.sem_inc(waited_pool, 1)
                for t in range(2):
                    for dst, c in ((zq, C_FOX), (zk, C_FOX + 256)):
                        pool.tensor_copy(dst[:, t, :, 0:HD],
                                         z[:, t, c:c + 256].rearrange("p (h d) -> p h d", h=H)
                                         ).then_inc(fox_staged, 1)
                pool.memset(zq[:, :, :, HD + 1:HD + 2], 1.0).then_inc(fox_staged, 1)
                pool.memset(zk[:, :, :, HD:HD + 1], 1.0).then_inc(fox_staged, 1)
                pool.wait_ge(ml_sq, at(l, 4, 4))
                pool.sem_inc(waited_pool, 1)
                pool.tensor_scalar(ssm[:, 0:2], ssm[:, 0:2], 1.0 / QR, EPS, ALU.mult, ALU.add).then_inc(ml_pool, 1)
                pool.tensor_scalar(ssm[:, 2:4], ssm[:, 2:4], 1.0 / KVR, EPS, ALU.mult, ALU.add
                                   ).then_inc(ml_pool, 1)
                pool.wait_ge(ml_pool, at(l, 4, 2))
                pool.tensor_tensor(rsm[:, 0:2], ssm[:, 0:2], half, ALU.pow).then_inc(ml_pool, 1)
                pool.tensor_tensor(rsm[:, 2:4], ssm[:, 2:4], half, ALU.pow).then_inc(ml_pool, 1)
                pool.wait_ge(p_in1.free0, at(l, 6, 3 + 6))
                pool.wait_ge(p_in1.free1, at(l, 6, 3 + 6))
                pool.wait_ge(tab_act, 4)
                for t in range(2):
                    v = z[:, t, C_DIL:C_DIL + 512].rearrange("p (h e d) -> p h e d", e=2, d=32)
                    flat = z[:, t, C_DIL:C_DIL + 512].rearrange("p (h d) -> p h d", d=32)
                    tmp = rt_dil.rearrange("p (h e d) -> p h e d", e=2, d=32)
                    tflat = rt_dil.rearrange("p (h d) -> p h d", d=32)

                    def wide(table):
                        return table[:, t, :].unsqueeze(1).broadcast_to([P, 16, 32])

                    if t:
                        pool.wait_ge(dil_rope, at(l, 8, 4))
                    pool.tensor_tensor(tflat, flat, wide(sinh), ALU.mult).then_inc(dil_rope, 1)
                    pool.tensor_tensor(flat, flat, wide(cosh), ALU.mult).then_inc(dil_rope, 1)
                    pool.wait_ge(dil_rope, at(l, 8, 4 * t + 2))
                    pool.tensor_tensor(v[:, :, 0, :], v[:, :, 0, :], tmp[:, :, 1, :], ALU.subtract
                                       ).then_inc(dil_rope, 1)
                    pool.tensor_tensor(v[:, :, 1, :], v[:, :, 1, :], tmp[:, :, 0, :], ALU.add
                                       ).then_inc(dil_rope, 1)
                output_rstd(l, n_mix1, 1.0)
                input_rstd(l, t_ffn1)
                output_rstd(l, n_ffn1, 1.0)

            with pool.Fori(0, LAYERS, 1) as l:
                input_rstd(l, t_f21)
                for j, n in enumerate(("ffn1_post_2", "mix_post_2", "ffn2_post_2")):
                    pool.dma_start(gp[j][:, :], A[n][l].partition_broadcast(P)).then_inc(gains_in[1], 16)
                pool.dma_start(bgate, A["b_gate_2"][l].partition_broadcast(P)).then_inc(gains_in[1], 16)
                output_rstd(l, n_f21, 0.5)
                input_rstd(l, t_mix2)
                pool.wait_ge(p_in2.free0, at(l, NC2, 3 + 6))
                pool.wait_ge(p_in2.free1, at(l, NC2, 3 + 6))
                for t in range(2):
                    pool.tensor_tensor(z2[:, t, DM:2 * DM], z2[:, t, DM:2 * DM], z2[:, t, 2 * DM:3 * DM],
                                       ALU.mult).then_inc(u_done, 1)
                pool.wait_ge(p_in2.free0, at(l, NC2, 3 + NC2))
                pool.wait_ge(p_in2.free1, at(l, NC2, 3 + NC2))
                pool.wait_ge(gains_in[1], at(l, 64, 64))
                for t in range(2):
                    pool.tensor_tensor(z2[:, t, 4 * DM:6 * DM], z2[:, t, 4 * DM:6 * DM], bgate, ALU.add
                                       ).then_inc(biased, 1)
                output_rstd(l, n_mix2, 1.0)
                input_rstd(l, t_f22)
                output_rstd(l, n_f22, 0.5)

        @block.scalar
        def _(act):
            act.sem_inc(p_in1.free0, 3)
            act.sem_inc(p_in2.free0, 3)

            def split(u, small=False):
                act.wait_ge(loaded[u.slot], u.turns * 32)
                act.wait_ge(unit_used, u.done)
                if small:
                    nc.scalar.activation(whi[u.slot][0:QRH, SM_Q:SLOTW], raw[u.slot][0:QRH, SM_Q:SLOTW], ACT.Copy)
                n = SM_Q if small else UNIT
                nc.scalar.activation(whi[u.slot][:, 0:n], raw[u.slot][:, 0:n], ACT.Copy).then_inc(hi_done, 1)

            def split_part(u, n):
                act.wait_ge(loaded[u.slot], u.turns * 32)
                act.wait_ge(unit_used, u.done)
                nc.scalar.activation(whi[u.slot][:, 0:n], raw[u.slot][:, 0:n], ACT.Copy).then_inc(hi_done, 1)

            def hi_pieces(l, tn, dst, gained):
                for i, (c, t) in enumerate(PIECES):
                    act.wait_ge(tn.gained if gained else tn.turned, at(tn.round(l), 4, i + 1))
                    src = stage[:, i % 2, :] if gained else T(i % 2)
                    nc.scalar.activation(dst[:, 4 * c:4 * c + 4, P * t:P * t + P],
                                         src.rearrange("p (k s) -> p k s", k=4), ACT.Copy).then_inc(tn.hi, 1)

            def square_x(l, tn, xv):
                act.wait_ge(x_ready, xv)
                for t in range(2):
                    nc.scalar.activation(junk[:, 2 * t:2 * t + 2, :], x[:, t, :].rearrange("p (c n) -> p c n", c=2),
                                         ACT.Square, accum_out=ssx[:, t:t + 1]).then_inc(tn.squared, 1)

            def square_y(l, pn, y_wait):
                for i, (c, t) in enumerate(PIECES):
                    y_wait(act, i)
                    nc.scalar.activation(junk[:, i, :], D(t, c), ACT.Square,
                                         accum_out=ssy[:, 2 * t + c:2 * t + c + 1]).then_inc(pn.squared, 1)

            def swiglu(units, k0, l, f, tn):
                b = [units(k0 + 1)]
                act.wait_ge(tn.rstd, at(tn.round(l), 1, 1))

                def silu(j, ub):
                    for t in range(2):
                        if t == 0:
                            act.wait_ge(f.gu, f.round(l) * NJ + j + 1)
                        else:
                            act.wait_ge(unit_used, ub.done + SLOTS)
                        nc.scalar.activation(gate[:, t, :], G(t, FC), ACT.Silu, scale=rsx[:, t:t + 1]
                                             ).then_inc(f.silu, 1)

                def hi(j):
                    for t in range(2):
                        act.wait_ge(f.turned, f.round(l) * (2 * NJ) + j * 2 + (t + 1))
                        nc.scalar.activation(f_hi[:, :, P * t:P * t + P],
                                             T(t, 256).rearrange("p (k s) -> p k s", k=2), ACT.Copy
                                             ).then_inc(f.hi, 1)

                split(units(k0 + 2))
                silu(0, units(k0 + 1))
                split(units(k0 + 3))
                hi(0)
                split(units(k0 + 4))
                with act.Fori(0, NJ - 2, 1) as i:
                    silu(i + 1, units(k0 + 3, i, 3))
                    split(units(k0 + 5, i, 3))
                    split(units(k0 + 6, i, 3))
                    hi(i + 1)
                    split(units(k0 + 7, i, 3))
                silu(NJ - 1, units(k0 + 3 * NJ - 3))
                split(units(k0 + 3 * NJ - 1))
                hi(NJ - 1)
                split(units(k0 + 3 * NJ))
                split(units(k0 + 3 * NJ + 1))

            def y_of_ffn(units, k0, l, f):
                def wait(eng, i):
                    if i < 3:
                        eng.wait_ge(f.y, at(f.round(l), 3, i + 1))
                    else:
                        eng.wait_ge(unit_used, units(k0 + 3 * NJ - 1).done + SLOTS)
                return wait

            def y_of_proj(units, k0, l, y):
                def wait(eng, i):
                    if i % 2 == 0:
                        eng.wait_ge(y, at(l, 2, i // 2 + 1))
                    else:
                        eng.wait_ge(unit_used, units(k0 + i).done + SLOTS)
                return wait

            for k in range(2):
                split(first_units(0)(k))
            act.wait_ge(tab, 12)
            nc.scalar.activation(sinh[:, :, :], Z[:, 1024:1088].rearrange("p (t d) -> p t d", t=2), ACT.Sin
                                 ).then_inc(tab_act, 1)
            nc.scalar.activation(cosh[:, :, :], Z[:, 1088:1152].rearrange("p (t d) -> p t d", t=2), ACT.Sin
                                 ).then_inc(tab_act, 1)
            act.wait_ge(tab_act, 2)
            even = "p t (d e) -> p t d e"
            nc.scalar.activation(sinr[:, :, :], sinh[:, :, :].rearrange(even, e=2)[:, :, :, 0], ACT.Copy
                                 ).then_inc(tab_act, 1)
            nc.scalar.activation(cosr[:, :, :], cosh[:, :, :].rearrange(even, e=2)[:, :, :, 0], ACT.Copy
                                 ).then_inc(tab_act, 1)

            with act.Fori(0, LAYERS, 1) as l:
                units = first_units(l)
                hi_pieces(l, t_mix1, a_hi, True)
                square_x(l, t_mix1, x1(l, 0))
                for c in range(NC1):
                    if c == NC1 - 1:
                        act.wait_ge(short_loaded, at(l, 16, 16))
                    split(units(2 * c + 2), small=(2 * c + 2 == U_SMALL))
                    split(units(2 * c + 3))
                    if c == 0:
                        act.wait_ge(t_mix1.rstd, at(t_mix1.round(l), 1, 1))
                    act.wait_ge(p_in1.t0, at(l, 6, c + 1))
                    nc.scalar.activation(z[:, 0, 512 * c:512 * c + 512], chunk_bank(c, 0), ACT.Copy,
                                         scale=rsx[:, 0:1]).then_inc(p_in1.free0, 1)
                act.wait_ge(p_in1.t0, at(l, 6, 6))
                nc.scalar.activation(z[:, 0, 512 * NC1:D_IN], chunk_bank(NC1, 0, REM), ACT.Copy,
                                     scale=rsx[:, 0:1]).then_inc(p_in1.free0, 1)
                split(units(12))
                act.wait_ge(p_in1.free0, at(l, 6, 3 + 6))
                act.wait_ge(p_in1.free1, at(l, 6, 3 + 6))
                for j, (c0, n) in enumerate(((C_CQ, QR), (C_CKV, KVR))):
                    for t in range(2):
                        nc.scalar.activation(junk[:, 2 * j + t, 0:n], z[:, t, c0:c0 + n], ACT.Square,
                                             accum_out=ssm[:, 2 * j + t:2 * j + t + 1]).then_inc(ml_sq, 1)
                act.wait_ge(fg_dve, at(l, 5, 2))
                nc.scalar.activation(fg[2], fg[1], ACT.Exp, scale=-1.0).then_inc(fg_act, 1)
                act.wait_ge(fg_dve, at(l, 5, 3))
                nc.scalar.activation(fg[3], fg[4], ACT.Ln).then_inc(fg_act, 1)

                def latent():
                    act.wait_ge(ml_turned, at(l, 2, 1))
                    nc.scalar.activation(b_hi[0:QRH, 0:2, :], T(0, 512, QRH).rearrange("p (k s) -> p k s", k=2),
                                         ACT.Copy).then_inc(ml_hi, 1)
                    act.wait_ge(ml_turned, at(l, 2, 2))
                    nc.scalar.activation(b_hi[:, 2, :], T(1, 256), ACT.Copy).then_inc(ml_hi, 1)
                    act.wait_ge(ml_q, at(l, 3, 1))
                    nc.scalar.activation(zq[:, 0, :, :], G(0, 384).rearrange("p (h d) -> p h d", h=H), ACT.Copy
                                         ).then_inc(ml_out0, 1)
                    act.wait_ge(ml_q, at(l, 3, 3))
                    kv = T(0).rearrange("p (h e d) -> p h e d", h=H, e=2)
                    nc.scalar.activation(zk[:, 0, :, 0:HD], kv[:, :, 0, :], ACT.Copy).then_inc(ml_out0, 1)
                    nc.scalar.activation(vm[:, 0, :, :], kv[:, :, 1, :], ACT.Copy).then_inc(ml_out0, 1)

                def attend(n):
                    if n < 4:
                        dq = KINDS[n][1]
                        for t in range(2):
                            act.wait_ge(qk_turned, at(l, 16, 4 * n + 2 * t + 1))
                            nc.scalar.activation(qT[0:dq, :, P * t:P * t + P],
                                                 T(0, 512, dq).rearrange("p (h s) -> p h s", h=H), ACT.Copy
                                                 ).then_inc(q_out, 1)
                    if n >= 1:
                        m = n - 1
                        for j, b in enumerate((0, 2)):
                            act.wait_ge(p_turned, at(l, 12, 3 * m + b + 1))
                            nc.scalar.activation(pT[b], T(0).rearrange("p (h s) -> p h s", h=H), ACT.Copy
                                                 ).then_inc(pT_act, 1)
                    if n < 4:
                        for qt in range(2):
                            act.wait_ge(neg_max, at(l, 8, 2 * n + qt + 1))
                            pr = probs[n % 2][qt]
                            for h in range(H):
                                i = 4 * qt + h
                                ins = nc.scalar.activation(pr[:, h, :], pr[:, h, :], ACT.Exp,
                                                           bias=nm[:, i:i + 1], accum_out=sums[:, i:i + 1])
                            ins.then_inc(p_ready, 1)

                attend(0)
                latent()
                for n in range(1, 5):
                    attend(n)
                hi_pieces(l, t_att, b_hi, False)
                for k in range(2, 6):
                    split(units(U_OUT + k))
                square_y(l, n_mix1, y_of_proj(units, U_OUT, l, y_out1))
                hi_pieces(l, t_ffn1, a_hi, True)
                square_x(l, t_ffn1, x1(l, 1))
                swiglu(units, U_FFN, l, f_1, t_ffn1)
                square_y(l, n_ffn1, y_of_ffn(units, U_FFN, l, f_1))

            with act.Fori(0, LAYERS, 1) as l:
                units = second_units(l)
                hi_pieces(l, t_f21, a_hi, True)
                square_x(l, t_f21, x2(l, 0))
                swiglu(units, V_FFN1, l, f_21, t_f21)
                square_y(l, n_f21, y_of_ffn(units, V_FFN1, l, f_21))
                hi_pieces(l, t_mix2, a_hi, True)
                square_x(l, t_mix2, x2(l, 1))
                act.wait_ge(t_mix2.rstd, at(t_mix2.round(l), 1, 1))
                with act.Fori(0, NC2 // 3, 1) as i:
                    for c in range(3):
                        for e in range(2):
                            k = V_IN + 2 * c + 2 + e
                            split(units(k, i, 6))
                        act.wait_ge(p_in2.t0, l * NC2 + i * 3 + (c + 1))
                        nc.scalar.activation(z2[:, 0, bass.ds(i * 1536 + 512 * c, 512)], chunk_bank(c, 0), ACT.Copy,
                                             scale=rsx[:, 0:1]).then_inc(p_in2.free0, 1)
                split_part(units(V_PG + 2), 512)
                for g in range(4):
                    act.wait_ge(pooled, at(l, 4, g + 1))
                    nc.scalar.activation(a_hi[:, 2 * g:2 * g + 2, :],
                                         T(g % 2).rearrange("p (k s) -> p k s", k=2), ACT.Copy).then_inc(d_hi, 1)
                for g in range(4):
                    act.wait_ge(yp_f, at(l, 8, 2 * g + 2))
                    nc.scalar.activation(b_hi[:, 2 * g:2 * g + 2, :],
                                         stage[:, g % 2, :].rearrange("p (k s) -> p k s", k=2), ACT.Copy
                                         ).then_inc(yp_hi, 1)
                    if g >= 2:
                        split(units(V_PO + g - 2))
                for i in range(8):
                    c, t = PIECES[i % 4]
                    act.wait_ge(ub_turned, at(l, 8, i + 1))
                    dst = quarter(c, (2 if i < 4 else 3) * DM)
                    nc.scalar.activation(dst[:, :, P * t:P * t + P], T(i % 2).rearrange("p (k s) -> p k s", k=4),
                                         ACT.Copy).then_inc(ub_out, 1)
                split(units(V_PO + 2))
                for t in range(2):
                    act.wait_ge(biased, at(l, 2, t + 1))
                    nc.scalar.activation(z2[:, t, 4 * DM:6 * DM], z2[:, t, 4 * DM:6 * DM], ACT.Sigmoid
                                         ).then_inc(sig_done, 1)
                split(units(V_PO + 3))
                for c in range(2):
                    act.wait_ge(conv, at(l, 8, 4 * c + 4))
                    nc.scalar.activation(a_hi[:, 4 * c:4 * c + 4, :], quarter(c, 0), ACT.Copy).then_inc(cv_hi, 1)
                for k in range(4, 8):
                    split(units(V_PO + k))
                split(units(V_PO + 8))
                split(units(V_PO + 9))
                hi_pieces(l, t_gated, b_hi, False)
                for k in range(2, 6):
                    split(units(V_WO + k))
                square_y(l, n_mix2, y_of_proj(units, V_WO, l, y_wo))
                hi_pieces(l, t_f22, a_hi, True)
                square_x(l, t_f22, x2(l, 2))
                swiglu(units, V_FFN2, l, f_22, t_f22)
                square_y(l, n_f22, y_of_ffn(units, V_FFN2, l, f_22))

        @block.vector
        def _(dve):
            dve.sem_inc(split_done, SLOTS)
            dve.sem_inc(p_in1.free1, 3)
            dve.sem_inc(p_in2.free1, 3)
            V = nc.vector

            def split(u, small=False):
                s = u.slot
                dve.wait_ge(hi_done, u.done)
                if small:
                    V.tensor_tensor(wlo[s][0:QRH, SM_Q:SLOTW], raw[s][0:QRH, SM_Q:SLOTW],
                                    whi[s][0:QRH, SM_Q:SLOTW].bitcast(F32), ALU.subtract)
                n = SM_Q if small else UNIT
                V.tensor_tensor(wlo[s][:, 0:n], raw[s][:, 0:n], whi[s][:, 0:n].bitcast(F32),
                                ALU.subtract).then_inc(split_done, 1)

            def split_part(u, n):
                s = u.slot
                dve.wait_ge(hi_done, u.done)
                V.tensor_tensor(wlo[s][:, 0:n], raw[s][:, 0:n], whi[s][:, 0:n].bitcast(F32),
                                ALU.subtract).then_inc(split_done, 1)

            def piece(buf, c, t):
                return buf[:, 4 * c:4 * c + 4, P * t:P * t + P]

            def lo_pieces(l, tn, hi, lo, gain):
                for i in range(5 if gain is not None else 4):
                    if gain is not None and i < 4:
                        c, t = PIECES[i]
                        dve.wait_ge(tn.turned, at(tn.round(l), 4, i + 1))
                        if i >= 2:
                            dve.wait_ge(tn.lo, at(tn.round(l), 4, i - 1))
                        V.tensor_tensor(stage[:, i % 2, :].rearrange("p (k s) -> p k s", k=4),
                                        T(i % 2).rearrange("p (k s) -> p k s", k=4),
                                        gain[:, 4 * c:4 * c + 4].unsqueeze(2).broadcast_to([P, 4, P]),
                                        ALU.mult).then_inc(tn.gained, 1)
                    j = i - 1 if gain is not None else i
                    if j >= 0:
                        c, t = PIECES[j]
                        src = stage[:, j % 2, :] if gain is not None else T(j % 2)
                        dve.wait_ge(tn.hi, at(tn.round(l), 4, j + 1))
                        V.tensor_tensor(piece(lo, c, t), src.rearrange("p (k s) -> p k s", k=4),
                                        piece(hi, c, t).bitcast(F32), ALU.subtract).then_inc(tn.lo, 1)

            def residual(l, pn, gains, xv):
                dve.wait_ge(pn.rstd, at(pn.round(l), 1, 1))
                for i in range(5):
                    if i < 4:
                        c, t = PIECES[i]
                        if i >= 2:
                            dve.wait_ge(x_ready, xv + (i - 1))
                        V.scalar_tensor_tensor(out=stage[:, i % 2, :], in0=D(t, c), scalar=rsy[:, t:t + 1],
                                               in1=gains[:, 512 * c:512 * c + 512], op0=ALU.mult, op1=ALU.mult
                                               ).then_inc(pn.scaled, 1)
                    if i >= 1:
                        c, t = PIECES[i - 1]
                        dve.wait_ge(pn.scaled, at(pn.round(l), 4, i))
                        xs = x[:, t, 512 * c:512 * c + 512]
                        V.tensor_tensor(xs, xs, stage[:, (i - 1) % 2, :], ALU.add).then_inc(x_ready, 1)
                dve.wait_ge(x_ready, xv + 4)

            def swiglu(units, k0, l, f, tn):
                dve.wait_ge(tn.rstd, at(tn.round(l), 1, 1))

                def mult(j):
                    for t in range(2):
                        dve.wait_ge(f.silu, f.round(l) * (2 * NJ) + j * 2 + (t + 1))
                        V.scalar_tensor_tensor(out=ffn[:, t, :], in0=G(t)[:, FC:2 * FC], scalar=rsx[:, t:t + 1],
                                               in1=gate[:, t, :], op0=ALU.mult, op1=ALU.mult).then_inc(f.f, 1)

                def lo(j):
                    for t in range(2):
                        dve.wait_ge(f.hi, f.round(l) * (2 * NJ) + j * 2 + (t + 1))
                        V.tensor_tensor(f_lo[:, :, P * t:P * t + P], T(t, 256).rearrange("p (k s) -> p k s", k=2),
                                        f_hi[:, :, P * t:P * t + P].bitcast(F32), ALU.subtract).then_inc(f.lo, 1)

                split(units(k0 + 2))
                mult(0)
                split(units(k0 + 3))
                lo(0)
                split(units(k0 + 4))
                with dve.Fori(0, NJ - 2, 1) as i:
                    mult(i + 1)
                    split(units(k0 + 5, i, 3))
                    split(units(k0 + 6, i, 3))
                    lo(i + 1)
                    split(units(k0 + 7, i, 3))
                mult(NJ - 1)
                split(units(k0 + 3 * NJ - 1))
                lo(NJ - 1)
                split(units(k0 + 3 * NJ))
                split(units(k0 + 3 * NJ + 1))

            for k in range(2):
                split(first_units(0)(k))

            ang = Z[:, 1152:1216].rearrange("p (t d) -> p t d", t=2)
            trn = Z[:, 1216:1280].rearrange("p (t d) -> p t d", t=2)
            red = Z[:, 1024:1088].rearrange("p (t d) -> p t d", t=2)
            cred = Z[:, 1088:1152].rearrange("p (t d) -> p t d", t=2)
            posf = Z[:, 1280:1282]
            dve.wait_ge(par_loaded, 9 * 16)
            dve.wait_ge(con, 36)
            V.tensor_copy(posf, posi[:, :]).then_inc(tab, 1)
            dve.wait_ge(tab, 1)
            V.tensor_tensor(ang, Z[:, 0:32].unsqueeze(1).broadcast_to([P, 2, 32]),
                            posf.unsqueeze(2).broadcast_to([P, 2, 32]), ALU.mult).then_inc(tab, 1)
            dve.wait_ge(tab, 2)
            magic = 1.5 * 2.0 ** 23
            V.tensor_scalar(trn, ang, 1.0 / (2 * np.pi), magic, ALU.mult, ALU.add).then_inc(tab, 1)
            dve.wait_ge(tab, 3)
            V.tensor_scalar(trn, trn, magic, None, ALU.subtract).then_inc(tab, 1)
            c1 = 6.28125
            c2 = float(np.float32(int((2 * np.pi - c1) * 2 ** 20) / 2 ** 20))
            c3 = 2 * np.pi - c1 - c2
            for j, cc in enumerate((c1, c2, c3)):
                dve.wait_ge(tab, 4 + j)
                V.scalar_tensor_tensor(out=ang, in0=trn, scalar=-cc, in1=ang, op0=ALU.mult, op1=ALU.add
                                       ).then_inc(tab, 1)
            dve.wait_ge(tab, 7)
            lim = float(np.nextafter(np.float32(np.pi), np.float32(0)))
            V.tensor_scalar(red, ang, lim, -lim, ALU.min, ALU.max).then_inc(tab, 1)
            dve.wait_ge(tab, 8)
            V.scalar_tensor_tensor(out=cred, in0=red, scalar=-1.0, in1=red, op0=ALU.mult, op1=ALU.max
                                   ).then_inc(tab, 1)
            dve.wait_ge(tab, 9)
            V.tensor_scalar(cred, cred, -1.0, float(np.pi / 2), ALU.mult, ALU.add).then_inc(tab, 3)

            def masks(l):
                low, ok = scratch[3].bitcast(I32), scratch[4]
                n = 15
                V.tensor_scalar(ok, dist, 0.0, None, ALU.is_ge).then_inc(mask_step, 1)
                V.tensor_scalar(dilc[:, :], dist, float(P), None, ALU.is_le).then_inc(mask_step, 1)
                for j, dil in enumerate((4, 16)):
                    V.tensor_scalar(low, dist, dil - 1, None, ALU.bitwise_and).then_inc(mask_step, 1)
                    dve.wait_ge(mask_step, at(l, n, 3 + 3 * j))
                    V.tensor_scalar(dilm[:, :], low, 0.0, None, ALU.is_equal).then_inc(mask_step, 1)
                    dve.wait_ge(mask_step, at(l, n, 4 + 3 * j))
                    V.tensor_tensor(dilc[:, :], dilc[:, :], dilm[:, :], ALU.add).then_inc(mask_step, 1)
                    dve.wait_ge(mask_step, at(l, n, 5 + 3 * j))
                V.tensor_tensor(dilc[:, :], dilc[:, :], ok, ALU.mult).then_inc(mask_step, 1)
                dve.wait_ge(mask_step, at(l, n, 9))
                V.tensor_scalar(dilm[:, :], dilc[:, :], 1.0, -1.0, ALU.min, ALU.add).then_inc(mask_step, 1)
                V.tensor_scalar(causal[:, :], ok, NEG, -NEG, ALU.mult, ALU.add).then_inc(mask_step, 1)
                dve.wait_ge(mask_step, at(l, n, 11))
                V.tensor_scalar(dilm[:, :], dilm[:, :], NEG, None, ALU.mult).then_inc(mask_step, 1)
                V.memset(upper[:, 1, :], 1.0).then_inc(mask_step, 1)
                V.tensor_scalar(upper[:, 0, :], back[:, 0:P], 0.0, None, ALU.is_ge).then_inc(mask_step, 1)
                V.tensor_scalar(scratch[5], back, 0.0, None, ALU.is_ge).then_inc(mask_step, 1)
                dve.wait_ge(mask_step, at(l, n, 15))

            def pooling_band(l, g):
                w, w0, w1, w2 = WINDOWS[g], scratch[5], scratch[6], scratch[7]
                n, b = 8 * len(WINDOWS), 8 * g
                V.tensor_scalar(w1, back, float(w), None, ALU.is_lt).then_inc(band_step, 1)
                V.tensor_scalar(w2[:, 0:P], count[:, 0:P], float(w), None, ALU.min).then_inc(band_step, 1)
                dve.wait_ge(band_step, at(l, n, b + 2))
                V.tensor_tensor(w1, w1, w0, ALU.mult).then_inc(band_step, 1)
                V.reciprocal(w2[:, 0:P], w2[:, 0:P]).then_inc(band_step, 1)
                dve.wait_ge(band_step, at(l, n, b + 4))
                V.tensor_tensor(band[:, g, 0:P], w1[:, 0:P], w2[:, 0:P], ALU.mult).then_inc(band_step, 1)
                V.tensor_scalar(band[:, g, P:S], w1[:, P:S], 1.0 / w, None, ALU.mult)
                V.tensor_scalar(band[:, g, S:384], w1[:, 0:P], 1.0 / w, None, ALU.mult).then_inc(band_step, 1)
                dve.wait_ge(band_step, at(l, n, b + 6))
                V.tensor_tensor(band[:, g, 0:P], band[:, g, 0:P], ident[:, :], ALU.subtract).then_inc(band_step, 1)
                V.tensor_tensor(band[:, g, S:384], band[:, g, S:384], ident[:, :], ALU.subtract
                                ).then_inc(band_step, 1)
                dve.wait_ge(band_step, at(l, n, b + 8))

            dve.wait_ge(par_turned, 2)
            V.tensor_copy(prm[:, 0:128], T(0, 128)).then_inc(par_ready, 1)
            V.tensor_copy(prm[:, 128:160], T(1, 32)).then_inc(par_ready, 1)
            dve.wait_ge(par_ready, 2)
            dve.wait_ge(tab_act, 4)
            dve.wait_ge(x_loaded, 16)
            dve.sem_inc(x_ready, 4)

            with dve.Fori(0, LAYERS, 1) as l:
                units = first_units(l)
                V.tensor_copy(cur[:, 0:8], prm[:, bass.ds(l * 8, 8)]).then_inc(cur_ready[0], 1)
                V.tensor_copy(cur[:, 8:16], prm[:, bass.ds(l * 8 + 32, 8)]).then_inc(cur_ready[0], 1)
                dve.wait_ge(cur_ready[0], at(l, 2, 2))
                lo_pieces(l, t_mix1, a_hi, a_lo, cur[:, 0:8])
                for c in range(NC1):
                    split(units(2 * c + 2), small=(2 * c + 2 == U_SMALL))
                    split(units(2 * c + 3))
                    if c == 0:
                        dve.wait_ge(t_mix1.rstd, at(t_mix1.round(l), 1, 1))
                    dve.wait_ge(unit_used, units(2 * c + 1).done + SLOTS)
                    V.tensor_scalar(z[:, 1, 512 * c:512 * c + 512], chunk_bank(c, 1), rsx[:, 1:2], None,
                                    ALU.mult).then_inc(p_in1.free1, 1)
                    if c == 0:
                        dve.wait_ge(iotas, at(l, 3, 3))
                        masks(l)
                    else:
                        pooling_band(l, c - 1)
                dve.wait_ge(s_done, at(l, 9, 1))
                V.tensor_scalar(z[:, 1, 512 * NC1:D_IN], chunk_bank(NC1, 1, REM), rsx[:, 1:2], None,
                                ALU.mult).then_inc(p_in1.free1, 1)
                split(units(12))
                dve.wait_ge(gains_in[0], at(l, 80, 80))
                dve.wait_ge(p_in1.free0, at(l, 6, 3 + 6))
                dve.wait_ge(p_in1.free1, at(l, 6, 3 + 6))
                V.tensor_tensor(fg[0], z[:, :, C_FG:C_FG + H], bfor[:, :].unsqueeze(1).broadcast_to([P, 2, H]),
                                ALU.add).then_inc(fg_dve, 1)
                dve.wait_ge(fg_dve, at(l, 5, 1))
                V.scalar_tensor_tensor(out=fg[1], in0=fg[0], scalar=-1.0, in1=fg[0], op0=ALU.mult, op1=ALU.max
                                       ).then_inc(fg_dve, 1)
                dve.wait_ge(fg_act, at(l, 2, 1))
                V.tensor_scalar(fg[4], fg[2], 1.0, None, ALU.add).then_inc(fg_dve, 1)
                dve.wait_ge(ml_pool, at(l, 4, 4))
                for j, (c0, w, g0) in enumerate(((C_CQ, QR, 0), (C_CKV, KVR, QR))):
                    for t in range(2):
                        V.scalar_tensor_tensor(out=z[:, t, c0:c0 + w], in0=z[:, t, c0:c0 + w],
                                               scalar=rsm[:, 2 * j + t:2 * j + t + 1], in1=gmla[:, g0:g0 + w],
                                               op0=ALU.mult, op1=ALU.mult).then_inc(ml_norm, 1)
                dve.wait_ge(fg_act, at(l, 2, 2))
                V.tensor_scalar(fg[1], fg[0], 0.0, None, ALU.min).then_inc(fg_dve, 1)
                dve.wait_ge(fg_dve, at(l, 5, 4))
                V.tensor_tensor(fg[0], fg[1], fg[3], ALU.subtract).then_inc(fg_dve, 1)
                dve.wait_ge(fg_sum, at(l, 1, 1))
                dve.wait_ge(fox_staged, at(l, 6, 6))
                cum = T(0, 8).rearrange("p (t h) -> p t h", t=2)
                V.tensor_scalar(zq[:, :, :, HD], cum, HD ** 0.5, None, ALU.mult).then_inc(fg_put, 1)
                V.tensor_scalar(zk[:, :, :, HD + 1], cum, -HD ** 0.5, None, ALU.mult).then_inc(fg_put, 1)

                def rotate(c0, tmps, done):
                    for t in range(2):
                        flat = z[:, t, c0:c0 + 512].rearrange("p (h d) -> p h d", d=32)
                        V.tensor_tensor(tmps[t].rearrange("p (h d) -> p h d", d=32), flat,
                                        sinh[:, t, :].unsqueeze(1).broadcast_to([P, 16, 32]), ALU.mult
                                        ).then_inc(done, 1)
                        V.tensor_tensor(flat, flat, cosh[:, t, :].unsqueeze(1).broadcast_to([P, 16, 32]),
                                        ALU.mult).then_inc(done, 1)
                    for t in range(2):
                        dve.wait_ge(done, at(l, 8, 2 * t + 2))
                        v = z[:, t, c0:c0 + 512].rearrange("p (h e d) -> p h e d", e=2, d=32)
                        w = tmps[t].rearrange("p (h e d) -> p h e d", e=2, d=32)
                        V.tensor_tensor(v[:, :, 0, :], v[:, :, 0, :], w[:, :, 1, :], ALU.subtract).then_inc(done, 1)
                        V.tensor_tensor(v[:, :, 1, :], v[:, :, 1, :], w[:, :, 0, :], ALU.add).then_inc(done, 1)

                def rotate_latent():
                    tm = rt_mla.rearrange("p (a t h d) -> p a t h d", a=2, t=2, h=H)
                    ck = cosr[:, :, :]
                    sk = sinr[:, :, :]

                    def bc(a):
                        return a.unsqueeze(2).broadcast_to([P, 2, H, 16])

                    qa, qb = zq[:, :, :, HD:HD + 16], zq[:, :, :, HD + 16:HD + 32]
                    V.tensor_tensor(tm[:, 0], qa, bc(sk), ALU.mult).then_inc(ml_rope, 1)
                    V.tensor_tensor(tm[:, 1], qb, bc(sk), ALU.mult).then_inc(ml_rope, 1)
                    V.tensor_tensor(qa, qa, bc(ck), ALU.mult).then_inc(ml_rope, 1)
                    V.tensor_tensor(qb, qb, bc(ck), ALU.mult).then_inc(ml_rope, 1)
                    dve.wait_ge(ml_rope, at(l, 13, 4))
                    V.tensor_tensor(qa, qa, tm[:, 1], ALU.subtract).then_inc(ml_rope, 1)
                    V.tensor_tensor(qb, qb, tm[:, 0], ALU.add).then_inc(ml_rope, 1)
                    ka, kb = z[:, :, C_KR:C_KR + 16], z[:, :, C_KR + 16:C_KR + 32]
                    dve.wait_ge(ml_rope, at(l, 13, 6))
                    V.tensor_tensor(tm[:, 0, :, 0, :], ka, sk, ALU.mult).then_inc(ml_rope, 1)
                    V.tensor_tensor(tm[:, 1, :, 0, :], kb, sk, ALU.mult).then_inc(ml_rope, 1)
                    V.tensor_tensor(ka, ka, ck, ALU.mult).then_inc(ml_rope, 1)
                    V.tensor_tensor(kb, kb, ck, ALU.mult).then_inc(ml_rope, 1)
                    dve.wait_ge(ml_rope, at(l, 13, 10))
                    V.tensor_tensor(ka, ka, tm[:, 1, :, 0, :], ALU.subtract).then_inc(ml_rope, 1)
                    V.tensor_tensor(kb, kb, tm[:, 0, :, 0, :], ALU.add).then_inc(ml_rope, 1)
                    dve.wait_ge(ml_rope, at(l, 13, 12))
                    V.tensor_copy(zk[:, :, :, HD:HD + ROPE_D],
                                  z[:, :, C_KR:C_KR + ROPE_D].unsqueeze(2).broadcast_to([P, 2, H, ROPE_D])
                                  ).then_inc(ml_rope, 1)

                def latent():
                    dve.wait_ge(ml_hi, at(l, 2, 1))
                    V.tensor_tensor(b_lo[0:QRH, 0:2, :], T(0, 512, QRH).rearrange("p (k s) -> p k s", k=2),
                                    b_hi[0:QRH, 0:2, :].bitcast(F32), ALU.subtract).then_inc(ml_lo, 1)
                    dve.wait_ge(ml_hi, at(l, 2, 2))
                    V.tensor_tensor(b_lo[:, 2, :], T(1, 256), b_hi[:, 2, :].bitcast(F32), ALU.subtract
                                    ).then_inc(ml_lo, 1)
                    dve.wait_ge(ml_q, at(l, 3, 2))
                    V.tensor_copy(zq[:, 1, :, :], G(1, 384).rearrange("p (h d) -> p h d", h=H)).then_inc(ml_out1, 1)
                    dve.wait_ge(unit_used, units(U_SMALL).done + SLOTS)
                    kv = T(1).rearrange("p (h e d) -> p h e d", h=H, e=2)
                    V.tensor_copy(zk[:, 1, :, 0:HD], kv[:, :, 0, :]).then_inc(ml_out1, 1)
                    V.tensor_copy(vm[:, 1, :, :], kv[:, :, 1, :]).then_inc(ml_out1, 1)
                    dve.wait_ge(ml_out0, at(l, 3, 3))
                    dve.wait_ge(ml_out1, at(l, 3, 3))
                    rotate_latent()

                def attend(n):
                    if n < 4:
                        name, dq, scale, _, _, _, mask, _ = KINDS[n]
                        for t in range(2):
                            dve.wait_ge(qk_turned, at(l, 16, 4 * n + 2 * t + 2))
                            V.tensor_copy(kT[0:dq, :, P * t:P * t + P],
                                          T(1, 512, dq).rearrange("p (h s) -> p h s", h=H)).then_inc(k_out, 1)
                        for qt in range(2):
                            nk = P * (qt + 1)
                            pr = probs[n % 2][qt]
                            dve.wait_ge(s_done, at(l, 9, 1 + 2 * n + qt + 1))
                            V.scalar_tensor_tensor(
                                out=pr, in0=scores_view(n, qt), scalar=scale,
                                in1=mask[:, S - nk:S].unsqueeze(1).broadcast_to([P, H, nk]),
                                op0=ALU.mult, op1=ALU.add).then_inc(masked, 1)
                            dve.wait_ge(masked, at(l, 8, 2 * n + qt + 1))
                            V.tensor_reduce(mx[:, 4 * qt:4 * qt + 4], pr, AX_X, ALU.max).then_inc(maxed, 1)
                            dve.wait_ge(maxed, at(l, 8, 2 * n + qt + 1))
                            if n >= 1:
                                dve.wait_ge(p_ready, at(l, 8, 2 * n - 1 + qt))
                            V.tensor_scalar(nm[:, 4 * qt:4 * qt + 4], mx[:, 4 * qt:4 * qt + 4], -1.0, None,
                                            ALU.mult).then_inc(neg_max, 1)
                    if n >= 1:
                        m = n - 1
                        dve.wait_ge(p_turned, at(l, 12, 3 * m + 2))
                        V.tensor_copy(pT[1], T(1).rearrange("p (h s) -> p h s", h=H)).then_inc(pT_dve, 1)
                        c0 = KINDS[m][7]
                        for qt in range(2):
                            dve.wait_ge(o_done, at(l, 8, 2 * m + qt + 1))
                            V.tensor_tensor(
                                z[:, qt, c0:c0 + H * HD].rearrange("p (h d) -> p h d", h=H), heads_out(m, qt),
                                rec[:, 4 * qt:4 * qt + 4].unsqueeze(2).broadcast_to([P, H, HD]), ALU.mult
                            ).then_inc(o_norm, 1)
                    if n < 4:
                        dve.wait_ge(p_ready, at(l, 8, 2 * n + 2))
                        if KINDS[n][0] == "dil":
                            for qt in range(2):
                                nk = P * (qt + 1)
                                pr = probs[n % 2][qt]
                                V.tensor_tensor(pr, pr, dilc[:, S - nk:S].unsqueeze(1).broadcast_to([P, H, nk]),
                                                ALU.mult).then_inc(dil_p, 1)
                            for qt in range(2):
                                dve.wait_ge(dil_p, at(l, 4, qt + 1))
                                V.tensor_reduce(sums[:, 4 * qt:4 * qt + 4], probs[n % 2][qt], AX_X, ALU.add
                                                ).then_inc(dil_p, 1)
                            dve.wait_ge(dil_p, at(l, 4, 4))
                        if n >= 1:
                            dve.wait_ge(o_norm, at(l, 8, 2 * n))
                        V.reciprocal(rec, sums).then_inc(recd, 1)
                        dve.wait_ge(recd, at(l, 4, n + 1))

                rotate(C_MOBA, rt, moba_rope)
                attend(0)
                latent()
                for n in range(1, 5):
                    attend(n)
                lo_pieces(l, t_att, b_hi, b_lo, None)
                for k in range(2, 6):
                    split(units(U_OUT + k))
                residual(l, n_mix1, gp[0], x1(l, 0))
                lo_pieces(l, t_ffn1, a_hi, a_lo, cur[:, 8:16])
                swiglu(units, U_FFN, l, f_1, t_ffn1)
                residual(l, n_ffn1, gp[1], x1(l, 1))

            with dve.Fori(0, LAYERS, 1) as l:
                units = second_units(l)
                for dst, src, n in ((0, 16, 8), (8, 48, 8), (16, 64, 8), (24, 80, 24), (48, 128, 8), (56, 144, 8)):
                    V.tensor_copy(cur[:, dst:dst + n], prm[:, bass.ds(l * n + src, n)]).then_inc(cur_ready[1], 1)
                dve.wait_ge(cur_ready[1], at(l, 6, 6))
                lo_pieces(l, t_f21, a_hi, a_lo, cur[:, 0:8])
                swiglu(units, V_FFN1, l, f_21, t_f21)
                dve.wait_ge(gains_in[1], at(l, 64, 64))
                residual(l, n_f21, gp[0], x2(l, 0))
                lo_pieces(l, t_mix2, a_hi, a_lo, cur[:, 8:16])
                with dve.Fori(0, NC2 // 3, 1) as i:
                    for c in range(3):
                        for e in range(2):
                            split(units(V_IN + 2 * c + 2 + e, i, 6))
                        if c == 0:
                            dve.wait_ge(t_mix2.rstd, at(t_mix2.round(l), 1, 1))
                        dve.wait_ge(unit_used, units(V_IN + 2 * c + 1, i, 6).done + SLOTS)
                        V.tensor_scalar(z2[:, 1, bass.ds(i * 1536 + 512 * c, 512)], chunk_bank(c, 1),
                                        rsx[:, 1:2], None, ALU.mult).then_inc(p_in2.free1, 1)
                split_part(units(V_PG + 2), 512)
                for g in range(4):
                    dve.wait_ge(d_hi, at(l, 4, g + 1))
                    V.tensor_tensor(a_lo[:, 2 * g:2 * g + 2, :], T(g % 2).rearrange("p (k s) -> p k s", k=2),
                                    a_hi[:, 2 * g:2 * g + 2, :].bitcast(F32), ALU.subtract).then_inc(d_lo, 1)
                for g in range(4):
                    if g == 0:
                        dve.wait_ge(pg_0, at(l, 1, 1))
                    else:
                        dve.wait_ge(unit_used, units(V_PG + g - 1).done + SLOTS)
                    for m in range(2):
                        k = 2 * g + m
                        V.tensor_scalar(stage[:, g % 2, 256 * m:256 * m + 256], G(g % 2)[:, 256 * m:256 * m + 256],
                                        cur[:, 48 + k:49 + k], cur[:, 56 + k:57 + k], ALU.add, ALU.mult
                                        ).then_inc(yp_f, 1)
                    dve.wait_ge(yp_hi, at(l, 4, g + 1))
                    V.tensor_tensor(b_lo[:, 2 * g:2 * g + 2, :],
                                    stage[:, g % 2, :].rearrange("p (k s) -> p k s", k=2),
                                    b_hi[:, 2 * g:2 * g + 2, :].bitcast(F32), ALU.subtract).then_inc(yp_lo, 1)
                    if g >= 2:
                        split(units(V_PO + g - 2))
                for c in range(2):
                    dve.wait_ge(ub_out, at(l, 8, 8))
                    src, dst, bg = quarter(c, 2 * DM), quarter(c, 0), quarter(c, 3 * DM)
                    for s in range(4):
                        if s:
                            dve.wait_ge(conv, at(l, 8, 4 * c + s))
                        for k in range(4):
                            kk = 4 * c + k
                            tap = 24 + 8 * (2 - s) + kk
                            if s == 0:
                                ins = V.tensor_scalar(dst[:, k, :], src[:, k, :], cur[:, tap:tap + 1], None, ALU.mult)
                            elif s < 3:
                                ins = V.scalar_tensor_tensor(
                                    out=dst[:, k, s:S], in0=src[:, k, 0:S - s], scalar=cur[:, tap:tap + 1],
                                    in1=dst[:, k, s:S], op0=ALU.mult, op1=ALU.add)
                            else:
                                ins = V.tensor_tensor(dst[:, k, :], dst[:, k, :], bg[:, k, :], ALU.mult)
                        ins.then_inc(conv, 1)
                    split(units(V_PO + 2 + c))
                for c in range(2):
                    dve.wait_ge(cv_hi, at(l, 2, c + 1))
                    V.tensor_tensor(a_lo[:, 4 * c:4 * c + 4, :], quarter(c, 0),
                                    a_hi[:, 4 * c:4 * c + 4, :].bitcast(F32), ALU.subtract).then_inc(cv_lo, 1)
                dve.wait_ge(sig_done, at(l, 2, 2))
                for c in range(2):
                    split(units(V_PO + 4 + 2 * c))
                    if c == 0:
                        split(units(V_PO + 5))
                    for t in range(2):
                        if t == 0:
                            dve.wait_ge(y_po, at(l, 2, c + 1))
                        else:
                            dve.wait_ge(unit_used, units(V_PO + 2 * c + 1).done + SLOTS)
                        zs = z2[:, t, 5 * DM + 512 * c:5 * DM + 512 * c + 512]
                        V.tensor_tensor(zs, D(t, c), zs, ALU.mult).then_inc(po_gated, 1)
                split(units(V_PO + 7))
                for c in range(2):
                    split(units(V_PO + 8 + c))
                    for t in range(2):
                        if t == 0:
                            dve.wait_ge(y_co, at(l, 2, c + 1))
                        else:
                            dve.wait_ge(unit_used, units(V_CO + 2 * c + 1).done + SLOTS)
                        i = 2 * c + t
                        zs = z2[:, t, 4 * DM + 512 * c:4 * DM + 512 * c + 512]
                        V.tensor_tensor(zs, D(t, c), zs, ALU.mult).then_inc(co_gated, 1)
                        dve.wait_ge(co_gated, at(l, 4, i + 1))
                        V.tensor_tensor(zs, zs, z2[:, t, 5 * DM + 512 * c:5 * DM + 512 * c + 512], ALU.add
                                        ).then_inc(mixed, 1)
                lo_pieces(l, t_gated, b_hi, b_lo, None)
                for k in range(2, 6):
                    split(units(V_WO + k))
                residual(l, n_mix2, gp[1], x2(l, 1))
                lo_pieces(l, t_f22, a_hi, a_lo, cur[:, 16:24])
                swiglu(units, V_FFN2, l, f_22, t_f22)
                residual(l, n_f22, gp[2], x2(l, 2))

        @block.tensor
        def _(pe):
            pe.sem_inc(unit_used, SLOTS)
            mm = nc.tensor.matmul

            def three(o, hi, lo, wh, wl, start, stop):
                mm(o, hi, wh, start=start, stop=False)
                mm(o, hi, wl, start=False, stop=False)
                return mm(o, lo, wh, start=False, stop=stop)

            def ready(u):
                pe.wait_ge(split_done, u.done + SLOTS)

            def turn(l, tn, src, src_ready, gained):
                for i, (c, t) in enumerate(PIECES):
                    src_ready(i)
                    if i >= 2:
                        pe.wait_ge(tn.gained if gained else tn.lo, at(tn.round(l), 4, i - 1))
                    for k in range(4):
                        ins = nc.tensor.transpose(T(i % 2)[:, P * k:P * k + P], src(4 * c + k, t), ident[:, :])
                    ins.then_inc(tn.turned, 1)

            def turn_x(l, tn, xv):
                def src_ready(i):
                    pe.wait_ge(x_ready, xv - 3 + i)
                turn(l, tn, lambda k, t: x[:, t, P * k:P * k + P], src_ready, True)

            def half_chunk(u, h, bank, hi, lo, lo_wait, n, t0_done, stop=True):
                ready(u)
                for t in range(2):
                    if lo_wait is not None:
                        lo_wait(h, t)
                    for k in range(4):
                        kk = 4 * h + k
                        ts = slice(P * t, P * t + P)
                        ws = slice(n * k, n * k + n)
                        ins = three(bank(t), hi[:, kk, ts], lo[:, kk, ts], whi[u.slot][:, ws], wlo[u.slot][:, ws],
                                    kk == 0, kk == NK - 1)
                    if t == 0 and h == 1 and t0_done is not None:
                        ins.then_inc(t0_done, 1)
                    if t == 1:
                        ins.then_inc(unit_used, 1)

            def project(units, k0, l, hi, lo, lo_wait, y, free=None):
                for c in range(2):
                    if free is not None:
                        free(c)
                    for h in range(2):
                        half_chunk(units(k0 + 2 * c + h), h, lambda t: D(t, c), hi, lo,
                                   lo_wait if c == 0 else None, 512, y)

            def pieces_lo(l, tn):
                return lambda h, t: pe.wait_ge(tn.lo, at(tn.round(l), 4, 2 * h + t + 1))

            def swiglu(units, k0, l, f, tn):
                def gate_up(j, ua, ub, first=False):
                    for h, u in enumerate((ua, ub)):
                        ready(u)
                        for t in range(2):
                            if first:
                                pe.wait_ge(tn.lo, at(tn.round(l), 4, 2 * h + t + 1))
                            elif h == 0:
                                pe.wait_ge(f.f, f.round(l) * (2 * NJ) + j * 2 + (t - 1))
                            for k in range(4):
                                kk = 4 * h + k
                                ts, ws = slice(P * t, P * t + P), slice(512 * k, 512 * k + 512)
                                ins = three(G(t), a_hi[:, kk, ts], a_lo[:, kk, ts], whi[u.slot][:, ws],
                                            wlo[u.slot][:, ws], kk == 0, kk == NK - 1)
                            if t == 1:
                                ins.then_inc(unit_used, 1)
                            elif h == 1:
                                ins.then_inc(f.gu, 1)

                def turn_f(j):
                    for t in range(2):
                        pe.wait_ge(f.f, f.round(l) * (2 * NJ) + j * 2 + (t + 1))
                        for k in range(2):
                            ins = nc.tensor.transpose(T(t)[:, P * k:P * k + P], ffn[:, t, P * k:P * k + P],
                                                      ident[:, :])
                        ins.then_inc(f.turned, 1)

                def down(j, u, start):
                    ready(u)
                    for t in range(2):
                        pe.wait_ge(f.lo, f.round(l) * (2 * NJ) + j * 2 + (t + 1))
                        for k in range(2):
                            for c in range(2):
                                ts, ws = slice(P * t, P * t + P), slice(DM * k + 512 * c, DM * k + 512 * c + 512)
                                st_ = start and k == 0
                                for a, w, s in ((f_hi, whi, st_), (f_hi, wlo, False), (f_lo, whi, False)):
                                    ins = mm(D(t, c), a[:, k, ts], w[u.slot][:, ws], start=s, stop=False,
                                             skip_group_check=True)
                    ins.then_inc(unit_used, 1)

                gate_up(0, units(k0), units(k0 + 1), first=True)
                turn_f(0)
                gate_up(1, units(k0 + 2), units(k0 + 3))
                down(0, units(k0 + 4), True)
                turn_f(1)
                with pe.Fori(0, NJ - 2, 1) as i:
                    gate_up(i + 2, units(k0 + 5, i, 3), units(k0 + 6, i, 3))
                    down(i + 1, units(k0 + 7, i, 3), False)
                    turn_f(i + 2)
                u = units(k0 + 3 * NJ - 1)
                ready(u)
                pe.wait_ge(f.lo, at(f.round(l), 2 * NJ, 2 * NJ))
                for i, (c, t) in enumerate(PIECES):
                    for k in range(2):
                        ts, ws = slice(P * t, P * t + P), slice(DM * k + 512 * c, DM * k + 512 * c + 512)
                        for a, w, s in ((f_hi, whi, 0), (f_hi, wlo, 0), (f_lo, whi, k == 1)):
                            ins = mm(D(t, c), a[:, k, ts], w[u.slot][:, ws], start=False, stop=bool(s),
                                     skip_group_check=True)
                    ins.then_inc(f.y if i < 3 else unit_used, 1)

            pe.wait_ge(con, 2)
            pe.wait_ge(par_loaded, 9 * 16)
            nc.tensor.transpose(T(0, 128), rows_a, ident[:, :]).then_inc(par_turned, 1)
            nc.tensor.transpose(T(1, 32), rows_b, ident[0:32, 0:32]).then_inc(par_turned, 1)
            pe.wait_ge(par_ready, 2)

            with pe.Fori(0, LAYERS, 1) as l:
                units = first_units(l)
                turn_x(l, t_mix1, x1(l, 0))
                for c in range(NC1):
                    pe.wait_ge(p_in1.free0, at(l, 6, c + 1))
                    pe.wait_ge(p_in1.free1, at(l, 6, c + 1))
                    for h in range(2):
                        half_chunk(units(2 * c + h), h, lambda t: chunk_bank(c, t), a_hi, a_lo,
                                   pieces_lo(l, t_mix1) if c == 0 else None, 512, p_in1.t0)
                u = units(U_SMALL)
                pe.wait_ge(p_in1.free0, at(l, 6, NC1 + 1))
                pe.wait_ge(p_in1.free1, at(l, 6, NC1 + 1))
                ready(u)
                for t in range(2):
                    for k in range(NK):
                        ts, ws = slice(P * t, P * t + P), slice(REM * k, REM * k + REM)
                        ins = three(chunk_bank(NC1, t, REM), a_hi[:, k, ts], a_lo[:, k, ts], whi[u.slot][:, ws],
                                    wlo[u.slot][:, ws], k == 0, k == NK - 1)
                    ins.then_inc(p_in1.t0 if t == 0 else s_done, 1)

                pe.wait_ge(fg_dve, at(l, 5, 5))
                mm(T(0)[:, 0:4], upper[:, 0, :], fg[0][:, 0, :], start=True, stop=True)
                mm(T(0)[:, 4:8], upper[:, 1, :], fg[0][:, 0, :], start=True, stop=False)
                mm(T(0)[:, 4:8], upper[:, 0, :], fg[0][:, 1, :], start=False, stop=True).then_inc(fg_sum, 1)

                def turn_qk(n):
                    name, dq, _, q, k, _, _, _ = KINDS[n]
                    if name == "fox":
                        pe.wait_ge(fg_put, at(l, 2, 2))
                    if name == "moba":
                        pe.wait_ge(moba_rope, at(l, 8, 8))
                        pe.wait_ge(ml_out0, at(l, 3, 3))
                        pe.wait_ge(ml_out1, at(l, 3, 3))
                    if name == "dil":
                        pe.wait_ge(dil_rope, at(l, 8, 8))
                    if name == "mla":
                        pe.wait_ge(ml_rope, at(l, 13, 13))
                    for t in range(2):
                        if t:
                            pe.wait_ge(q_out, at(l, 8, 2 * n + 1))
                        pe.sem_inc(waited_pe, 1)
                        for h in range(H):
                            ins = nc.tensor.transpose(T(0, 512, dq)[:, P * h:P * h + P], q(t, h), ident[:, :])
                        ins.then_inc(qk_turned, 1)
                        if t:
                            pe.wait_ge(k_out, at(l, 8, 2 * n + 1))
                        pe.sem_inc(waited_pe, 1)
                        for h in range(H):
                            ins = nc.tensor.transpose(T(1, 512, dq)[:, P * h:P * h + P], k(t, h), ident[:, :])
                        ins.then_inc(qk_turned, 1)

                def scores(n):
                    dq = KINDS[n][1]
                    for qt in range(2):
                        pe.wait_ge(q_out, at(l, 8, 2 * n + qt + 1))
                        pe.wait_ge(k_out, at(l, 8, 2 * n + qt + 1))
                        if n >= 2:
                            pe.wait_ge(o_norm, at(l, 8, 2 * (n - 2) + qt + 1))
                        for h in range(H):
                            ins = mm(scores_view(n, qt)[:, h, :], qT[0:dq, h, P * qt:P * qt + P],
                                     kT[0:dq, h, 0:P * (qt + 1)], start=True, stop=True)
                        ins.then_inc(s_done, 1)

                def values(n):
                    name, _, _, _, _, v, _, _ = KINDS[n]
                    pr = probs[n % 2]
                    if name == "dil":
                        pe.wait_ge(dil_p, at(l, 4, 4))
                    for b, (src, k0) in enumerate(((pr[0], 0), (pr[1], 0), (pr[1], P))):
                        pe.wait_ge(p_ready, at(l, 8, 2 * n + (1 if b == 0 else 2)))
                        if b == 2:
                            pe.wait_ge(pT_act, at(l, 8, 2 * n + 1))
                        for h in range(H):
                            ins = nc.tensor.transpose(T(b % 2)[:, P * h:P * h + P], src[:, h, k0:k0 + P], ident[:, :])
                        ins.then_inc(p_turned, 1)
                    for h in range(H):
                        ins = mm(heads_out(n, 0)[:, h, :], pT[0][:, h, :], v(0, h), start=True, stop=True)
                    ins.then_inc(o_done, 1)
                    pe.wait_ge(pT_dve, at(l, 4, n + 1))
                    pe.wait_ge(pT_act, at(l, 8, 2 * n + 2))
                    for h in range(H):
                        mm(heads_out(n, 1)[:, h, :], pT[1][:, h, :], v(0, h), start=True, stop=False)
                        ins = mm(heads_out(n, 1)[:, h, :], pT[2][:, h, :], v(1, h), start=False, stop=True)
                    ins.then_inc(o_done, 1)

                def latent():
                    pe.wait_ge(ml_norm, at(l, 4, 4))
                    pe.wait_ge(q_out, at(l, 8, 2))
                    pe.wait_ge(k_out, at(l, 8, 2))
                    for k in range(2):
                        for t in range(2):
                            ins = nc.tensor.transpose(T(0, 512, QRH)[:, S * k + P * t:S * k + P * t + P],
                                                      z[:, t, C_CQ + QRH * k:C_CQ + QRH * k + QRH], ident[:, :])
                    ins.then_inc(ml_turned, 1)
                    for t in range(2):
                        ins = nc.tensor.transpose(T(1)[:, P * t:P * t + P], z[:, t, C_CKV:C_CKV + KVR], ident[:, :])
                    ins.then_inc(ml_turned, 1)
                    s = u.slot
                    pe.wait_ge(ml_lo, at(l, 2, 1))
                    for t in range(2):
                        for k in range(2):
                            ts = slice(P * t, P * t + P)
                            ws = slice(SM_Q + 384 * k, SM_Q + 384 * k + 384)
                            ins = three(G(t, 384), b_hi[0:QRH, k, ts], b_lo[0:QRH, k, ts], whi[s][0:QRH, ws],
                                        wlo[s][0:QRH, ws], k == 0, k == 1)
                        ins.then_inc(ml_q, 1)
                    pe.wait_ge(ml_lo, at(l, 2, 2))
                    for t in range(2):
                        ts = slice(P * t, P * t + P)
                        ins = three(T(t), b_hi[:, 2, ts], b_lo[:, 2, ts], whi[s][:, SM_KV:SM_Q],
                                    wlo[s][:, SM_KV:SM_Q], True, True)
                        ins.then_inc(ml_q if t == 0 else unit_used, 1)

                turn_qk(0)
                scores(0)
                latent()
                for n in range(1, 4):
                    turn_qk(n)
                    scores(n)
                    values(n - 1)
                values(3)
                turn(l, t_att, lambda k, t: z[:, t, MIX_COLS[k]:MIX_COLS[k] + P],
                     lambda i: pe.wait_ge(o_norm, at(l, 8, 8)), False)
                project(units, U_OUT, l, b_hi, b_lo, pieces_lo(l, t_att), y_out1)
                turn_x(l, t_ffn1, x1(l, 1))
                swiglu(units, U_FFN, l, f_1, t_ffn1)

            with pe.Fori(0, LAYERS, 1) as l:
                units = second_units(l)
                turn_x(l, t_f21, x2(l, 0))
                swiglu(units, V_FFN1, l, f_21, t_f21)
                turn_x(l, t_mix2, x2(l, 1))
                with pe.Fori(0, NC2 // 3, 1) as i:
                    for c in range(3):
                        pe.wait_ge(p_in2.free0, l * NC2 + i * 3 + (c + 1))
                        pe.wait_ge(p_in2.free1, l * NC2 + i * 3 + (c + 1))
                        for h in range(2):
                            half_chunk(units(V_IN + 2 * c + h, i, 6), h, lambda t: chunk_bank(c, t), a_hi, a_lo,
                                       pieces_lo(l, t_mix2) if c == 0 else None, 512, p_in2.t0)
                pe.wait_ge(p_in2.free0, at(l, NC2, 3 + 8))
                pe.wait_ge(p_in2.free1, at(l, NC2, 3 + 8))
                for g in range(4):
                    if g >= 2:
                        pe.wait_ge(d_lo, at(l, 4, g - 1))
                    for m in range(2):
                        c0 = 3 * DM + P * (2 * g + m)
                        o = T(g % 2)[:, S * m:S * m + S]
                        mm(o, z2[:, 0, c0:c0 + P], band[:, g, 0:S], start=True, stop=True)
                        ins = mm(o[:, P:S], z2[:, 1, c0:c0 + P], band[:, g, S:384], start=False, stop=True,
                                 skip_group_check=True)
                    ins.then_inc(pooled, 1)
                pe.wait_ge(p_in2.free0, at(l, NC2, 3 + NC2))
                pe.wait_ge(p_in2.free1, at(l, NC2, 3 + NC2))
                for g in range(4):
                    u = units(V_PG + max(g - 1, 0))
                    ready(u)
                    pe.wait_ge(d_lo, at(l, 4, g + 1))
                    if g >= 2:
                        pe.wait_ge(yp_f, at(l, 8, 2 * (g - 1)))
                    for m in range(2):
                        for k in range(2):
                            c0 = (512 if g == 1 else 0) + 256 * k + P * m
                            o = G(g % 2)[:, S * m:S * m + S]
                            wh, wl = whi[u.slot][:, c0:c0 + P], wlo[u.slot][:, c0:c0 + P]
                            mm(o, wh, a_hi[:, 2 * g + k, :], start=k == 0, stop=False)
                            mm(o, wh, a_lo[:, 2 * g + k, :], start=False, stop=False)
                            ins = mm(o, wl, a_hi[:, 2 * g + k, :], start=False, stop=k == 1)
                    ins.then_inc(pg_0 if g == 0 else unit_used, 1)
                pe.wait_ge(u_done, at(l, 2, 2))
                for i in range(8):
                    c, t = PIECES[i % 4]
                    if i >= 2:
                        pe.wait_ge(ub_out, at(l, 8, i - 1))
                    for k in range(4):
                        c0 = (DM if i < 4 else 0) + P * (4 * c + k)
                        ins = nc.tensor.transpose(T(i % 2)[:, P * k:P * k + P], z2[:, t, c0:c0 + P], ident[:, :])
                    ins.then_inc(ub_turned, 1)
                project(units, V_PO, l, b_hi, b_lo, lambda h, t: pe.wait_ge(yp_lo, at(l, 4, 2 * h + 2)), y_po)

                def po_left(c):
                    pe.wait_ge(po_gated, at(l, 4, 2 * c + 2))
                project(units, V_CO, l, a_hi, a_lo, lambda h, t: pe.wait_ge(cv_lo, at(l, 2, h + 1)), y_co, po_left)
                turn(l, t_gated, lambda k, t: z2[:, t, 4 * DM + P * k:4 * DM + P * k + P],
                     lambda i: pe.wait_ge(mixed, at(l, 4, i + 1)), False)
                project(units, V_WO, l, b_hi, b_lo, pieces_lo(l, t_gated), y_wo)
                turn_x(l, t_f22, x2(l, 2))
                swiglu(units, V_FFN2, l, f_22, t_f22)


_INS = ["x", "positions", "w_in", "b_forget", "g_mla_q", "w_mla_q_up", "g_mla_kv", "w_mla_kv_up", "w_out",
        "g_pre_mix", "g_post_mix", "w_gate", "w_up", "w_down", "g_pre_ffn", "g_post_ffn", "ffn1_pre_2",
        "ffn1_post_2", "ffn1_w_gate_up_2", "ffn1_w_down_2", "mix_pre_2", "mix_post_2", "w_in_2", "b_gate_2",
        "conv_w_2", "w_conv_out_2", "w_pool_group_2", "b_pool_group_2", "pool_scale_2", "w_pool_out_2",
        "w_o_2", "ffn2_pre_2", "ffn2_post_2", "ffn2_w_gate_up_2", "ffn2_w_down_2"]


def kernel(**inputs):
    import concourse.bacc as bacc
    from concourse.bass_utils import run_bass_kernel_spmd

    nc = bacc.Bacc("TRN2", target_bir_lowering=False, num_devices=1)
    arrays, args = {}, {}
    for name in _INS:
        a = np.ascontiguousarray(inputs[name])
        arrays[f"in_{name}"] = a
        args[name] = nc.dram_tensor(f"in_{name}", a.shape, mybir.dt.from_np(a.dtype), kind="ExternalInput").ap()
    out = nc.dram_tensor("out_x", (1, S, DM), F32, kind="ExternalOutput").ap()
    build(nc, args, out)
    r = run_bass_kernel_spmd(nc, [arrays], core_ids=[0])
    return r.results[0]["out_x"]
```
